# Optimizing a Trainium2 kernel written in Bass

```python
import jax
import jax.numpy as jnp
from jax import lax
import numpy as np
import math
import jax, jax.numpy as jnp

D_MODEL = 1024
BATCH = 1
SEQ = 512
DEPTH = 2

D_MIX = 1024
M_HEADS = 4
M_HEAD_DIM = 96
M_WIDTH = M_HEADS * M_HEAD_DIM
M_CHUNK = 128
CONV_WIDTH = 4
A_HEADS = 6
A_NOPE = 64
A_ROPE = 32
A_QK_DIM = A_NOPE + A_ROPE
A_V_DIM = 64
A_WIDTH = A_HEADS * A_V_DIM
A_Q_RANK = 256
A_KV_RANK = 128
ROPE_THETA = 10000.0
Q_BLOCK = 128
C_GROUPS = 4
C_GROUP_DIM = 64
C_WIDTH = C_GROUPS * C_GROUP_DIM
C_CHUNK = 128
IN_SIZES = (M_WIDTH, M_WIDTH, M_WIDTH, M_WIDTH, M_HEADS, M_HEADS,
            A_Q_RANK, A_KV_RANK, A_ROPE, C_WIDTH, C_WIDTH)
D_IN = 4 * M_WIDTH + 2 * M_HEADS + A_Q_RANK + A_KV_RANK + A_ROPE + 2 * C_WIDTH
N_GROUPS = 4
EXPERTS_PER_GROUP = 8
N_EXPERTS = N_GROUPS * EXPERTS_PER_GROUP
TOP_K = 2
D_EXPERT = 256
MOE_BLOCK = 256
EPS = 1e-6


def rms_norm(x, gain):
    xf = x.astype(jnp.float32)
    y = xf * lax.rsqrt(jnp.mean(xf * xf, axis=-1, keepdims=True) + EPS)
    return (y * gain.astype(jnp.float32)).astype(x.dtype)

def head_rms_norm(x, gain, n_heads):
    b, s, w = x.shape
    y = rms_norm(x.reshape(b, s, n_heads, w // n_heads), gain.reshape(n_heads, w // n_heads))
    return y.reshape(b, s, w)

def split_cols(t, sizes):
    out, off = [], 0
    for size in sizes:
        out.append(t[..., off:off + size])
        off += size
    return out

def causal_depthwise_conv(x, w, b):
    width, seq = w.shape[0], x.shape[1]
    xp = jnp.pad(x, ((0, 0), (width - 1, 0), (0, 0)))
    y = b
    for j in range(width):
        y = y + xp[:, j:j + seq] * w[j]
    return y

def mlstm_chunkwise(q, k, v, i_pre, f_pre):
    B, S, H, Dh = q.shape
    L = M_CHUNK
    N = S // L
    f32 = jnp.float32
    def to_chunks(t):
        return t.astype(f32).reshape(B, N, L, H, -1).transpose(1, 0, 3, 2, 4)
    qc = to_chunks(q)
    kc = to_chunks(k) * (Dh ** -0.5)
    vc = to_chunks(v)
    log_f = jax.nn.log_sigmoid(f_pre.astype(f32)).reshape(B, N, L, H).transpose(1, 0, 3, 2)
    log_i = i_pre.astype(f32).reshape(B, N, L, H).transpose(1, 0, 3, 2)
    bcum = jnp.cumsum(log_f, axis=-1)
    causal = jnp.tril(jnp.ones((L, L), dtype=bool))

    def step(carry, inp):
        C, n, m = carry
        qt, kt, vt, bt, it = inp
        d = bt[..., :, None] - bt[..., None, :] + it[..., None, :]
        d = jnp.where(causal, d, -jnp.inf)
        inter = bt + m[..., None]
        m_row = jnp.maximum(inter, jnp.max(d, axis=-1))
        w_intra = jnp.exp(d - m_row[..., None])
        w_inter = jnp.exp(inter - m_row)
        s = jnp.einsum('bhld,bhsd->bhls', qt, kt) * w_intra
        num = (jnp.einsum('bhls,bhsd->bhld', s, vt)
               + w_inter[..., None] * jnp.einsum('bhvk,bhlk->bhlv', C, qt))
        den = jnp.sum(s, axis=-1) + w_inter * jnp.einsum('bhk,bhlk->bhl', n, qt)
        h = num / jnp.maximum(jnp.abs(den), jnp.exp(-m_row))[..., None]
        b_last = bt[..., -1]
        g = b_last[..., None] - bt + it
        m_new = jnp.maximum(b_last + m, jnp.max(g, axis=-1))
        a = jnp.exp(b_last + m - m_new)
        wg = jnp.exp(g - m_new[..., None])
        C_new = a[..., None, None] * C + jnp.einsum('bhs,bhsv,bhsk->bhvk', wg, vt, kt)
        n_new = a[..., None] * n + jnp.einsum('bhs,bhsk->bhk', wg, kt)
        return (C_new, n_new, m_new), h

    init = (jnp.zeros((B, H, Dh, Dh), f32), jnp.zeros((B, H, Dh), f32), jnp.zeros((B, H), f32))
    _, h = lax.scan(step, init, (qc, kc, vc, bcum, log_i))
    return h.transpose(1, 0, 3, 2, 4).reshape(B, S, H, Dh).astype(v.dtype)

def rope_tables(positions):
    inv_freq = 1.0 / (ROPE_THETA ** (jnp.arange(0, A_ROPE, 2, dtype=jnp.float32) / A_ROPE))
    ang = positions.astype(jnp.float32)[..., None] * inv_freq
    return jnp.cos(ang), jnp.sin(ang)

def apply_rope(x, cos, sin):
    half = x.shape[-1] // 2
    xf = x.astype(jnp.float32)
    c, s = cos[:, :, None, :], sin[:, :, None, :]
    x1, x2 = xf[..., :half], xf[..., half:]
    return jnp.concatenate([x1 * c - x2 * s, x1 * s + x2 * c], axis=-1).astype(x.dtype)

def causal_block_attention(q, k, v):
    B, S, H, Dq = q.shape
    nb = S // Q_BLOCK
    scale = Dq ** -0.5
    qb = q.reshape(B, nb, Q_BLOCK, H, Dq).transpose(1, 0, 2, 3, 4)
    kpos = jnp.arange(S)

    def one_block(args):
        qi, idx = args
        s = jnp.einsum('blhd,bshd->bhls', qi, k, preferred_element_type=jnp.float32) * scale
        qpos = idx * Q_BLOCK + jnp.arange(Q_BLOCK)
        s = jnp.where(kpos[None, :] <= qpos[:, None], s, -jnp.inf)
        p = jax.nn.softmax(s, axis=-1).astype(v.dtype)
        return jnp.einsum('bhls,bshd->blhd', p, v)

    o = lax.map(one_block, (qb, jnp.arange(nb)))
    return o.transpose(1, 0, 2, 3, 4).reshape(B, S, H, v.shape[-1])

def mla_mixer(c_q, c_kv, k_rope, cos, sin, q_gain, kv_gain, w_uq, w_ukv, qh_gain, kh_gain):
    B, S, _ = c_q.shape
    q = (rms_norm(c_q, q_gain) @ w_uq).reshape(B, S, A_HEADS, A_QK_DIM)
    kv = (rms_norm(c_kv, kv_gain) @ w_ukv).reshape(B, S, A_HEADS, A_NOPE + A_V_DIM)
    k_nope, v = kv[..., :A_NOPE], kv[..., A_NOPE:]
    k = jnp.concatenate([k_nope, jnp.broadcast_to(k_rope[:, :, None, :], (B, S, A_HEADS, A_ROPE))], axis=-1)
    q = rms_norm(q, qh_gain)
    k = rms_norm(k, kh_gain)
    q = jnp.concatenate([q[..., :A_NOPE], apply_rope(q[..., A_NOPE:], cos, sin)], axis=-1)
    k = jnp.concatenate([k[..., :A_NOPE], apply_rope(k[..., A_NOPE:], cos, sin)], axis=-1)
    o = causal_block_attention(q, k, v)
    return o.reshape(B, S, A_WIDTH)

def chunk_spatial_gating(u, v, v_gain, w_s, b_s):
    B, S, _ = u.shape
    n = S // C_CHUNK
    v = rms_norm(v.reshape(B, S, C_GROUPS, C_GROUP_DIM), v_gain.reshape(C_GROUPS, C_GROUP_DIM))
    vc = v.reshape(B, n, C_CHUNK, C_GROUPS, C_GROUP_DIM)
    w = w_s * jnp.tril(jnp.ones((C_CHUNK, C_CHUNK), dtype=w_s.dtype))
    mixed = jnp.einsum('gts,bnsgd->bntgd', w, vc) + b_s.T[None, None, :, :, None]
    return u * mixed.reshape(B, S, C_WIDTH)

def hier_moe(x, w_group, b_group, w_expert, b_expert, w1, w3, w2):
    B, S, D = x.shape
    T = B * S
    xt = x.reshape(T, D)
    f32 = jnp.float32
    g_logits = (xt @ w_group).astype(f32)
    g_prob = jax.nn.softmax(g_logits, axis=-1)
    _, g_sel = lax.top_k(g_logits + b_group.astype(f32), 1)
    g_sel = g_sel[:, 0]
    tok = jnp.arange(T)
    g_gate = g_prob[tok, g_sel]
    e_logits = (xt @ w_expert).astype(f32).reshape(T, N_GROUPS, EXPERTS_PER_GROUP)
    e_logits = e_logits[tok, g_sel]
    e_bias = b_expert.astype(f32).reshape(N_GROUPS, EXPERTS_PER_GROUP)[g_sel]
    e_prob = jax.nn.softmax(e_logits, axis=-1)
    _, e_local = lax.top_k(e_logits + e_bias, TOP_K)
    e_w = jnp.take_along_axis(e_prob, e_local, axis=1)
    e_w = e_w / jnp.sum(e_w, axis=-1, keepdims=True)
    weights = g_gate[:, None] * e_w
    expert_id = g_sel[:, None] * EXPERTS_PER_GROUP + e_local

    A = T * TOP_K
    flat_e = expert_id.reshape(A)
    flat_tok = jnp.arange(A, dtype=jnp.int32) // TOP_K
    flat_w = weights.reshape(A)
    order = jnp.argsort(flat_e)
    se, stok, sw = flat_e[order], flat_tok[order], flat_w[order]
    counts = jnp.bincount(flat_e, length=N_EXPERTS)
    starts = jnp.cumsum(counts) - counts
    padded = ((counts + MOE_BLOCK - 1) // MOE_BLOCK) * MOE_BLOCK
    pad_ends = jnp.cumsum(padded)
    pad_starts = pad_ends - padded
    dest = pad_starts[se] + jnp.arange(A) - starts[se]
    n_blocks = -(-A // MOE_BLOCK) + N_EXPERTS
    P = n_blocks * MOE_BLOCK
    row_tok = jnp.full((P,), T, dtype=jnp.int32).at[dest].set(stok)
    row_w = jnp.zeros((P,), dtype=x.dtype).at[dest].set(sw.astype(x.dtype))
    block_start = jnp.arange(n_blocks) * MOE_BLOCK
    block_e = jnp.minimum(jnp.sum(pad_ends[None, :] <= block_start[:, None], axis=1), N_EXPERTS - 1)
    x_pad = jnp.concatenate([xt, jnp.zeros((1, D), dtype=x.dtype)], axis=0)

    def expert_block(args):
        rows, rw, e = args
        xi = x_pad[rows]
        h = jax.nn.silu(xi @ w1[e]) * (xi @ w3[e])
        return (h @ w2[e]) * rw[:, None]

    yb = lax.map(expert_block, (row_tok.reshape(n_blocks, MOE_BLOCK), row_w.reshape(n_blocks, MOE_BLOCK), block_e))
    out = jnp.zeros((T + 1, D), dtype=x.dtype).at[row_tok].add(yb.reshape(P, D))[:T]
    return out.reshape(B, S, D)

def first_inputs(seed: int = 0) -> dict:
    key = jax.random.key(seed)
    ks = jax.random.split(key, 32)
    nrm = jax.random.normal
    def gain(k, n):
        return 1.0 + 0.02 * nrm(k, (DEPTH, n), jnp.float32)
    x = nrm(ks[0], (BATCH, SEQ, D_MODEL), jnp.float32)
    offsets = jax.random.randint(ks[1], (BATCH, 1), 0, 4096, dtype=jnp.int32)
    positions = offsets + jnp.arange(SEQ, dtype=jnp.int32)[None, :]
    f_bias = jnp.linspace(3.0, 6.0, M_HEADS, dtype=jnp.float32)[None, :]
    m_gate_bias = jnp.concatenate([0.1 * nrm(ks[6], (DEPTH, M_HEADS), jnp.float32),
                                   f_bias + 0.1 * nrm(ks[7], (DEPTH, M_HEADS), jnp.float32)], axis=-1)
    return {
        'x': x,
        'positions': positions,
        'attn_norm': gain(ks[2], D_MODEL),
        'w_in': nrm(ks[3], (DEPTH, D_MODEL, D_IN), jnp.float32) * D_MODEL ** -0.5,
        'm_conv_w': nrm(ks[4], (DEPTH, CONV_WIDTH, 2 * M_WIDTH), jnp.float32) * CONV_WIDTH ** -0.5,
        'm_conv_b': 0.02 * nrm(ks[5], (DEPTH, 2 * M_WIDTH), jnp.float32),
        'm_gate_bias': m_gate_bias,
        'a_q_norm': gain(ks[8], A_Q_RANK),
        'a_kv_norm': gain(ks[9], A_KV_RANK),
        'a_w_uq': nrm(ks[10], (DEPTH, A_Q_RANK, A_HEADS * A_QK_DIM), jnp.float32) * A_Q_RANK ** -0.5,
        'a_w_ukv': nrm(ks[11], (DEPTH, A_KV_RANK, A_HEADS * (A_NOPE + A_V_DIM)), jnp.float32) * A_KV_RANK ** -0.5,
        'a_q_head_norm': gain(ks[12], A_QK_DIM),
        'a_k_head_norm': gain(ks[13], A_QK_DIM),
        'c_v_norm': gain(ks[14], C_WIDTH),
        'c_w_s': nrm(ks[15], (DEPTH, C_GROUPS, C_CHUNK, C_CHUNK), jnp.float32) * C_CHUNK ** -0.5,
        'c_b_s': 1.0 + 0.1 * nrm(ks[16], (DEPTH, C_GROUPS, C_CHUNK), jnp.float32),
        'mix_out_norm': gain(ks[17], D_MIX),
        'w_out': nrm(ks[18], (DEPTH, D_MIX, D_MODEL), jnp.float32) * (D_MIX ** -0.5) * ((2 * DEPTH) ** -0.5),
        'ffn_norm': gain(ks[19], D_MODEL),
        'w_group': nrm(ks[20], (DEPTH, D_MODEL, N_GROUPS), jnp.float32) * D_MODEL ** -0.5,
        'b_group': 0.01 * nrm(ks[21], (DEPTH, N_GROUPS), jnp.float32),
        'w_expert': nrm(ks[22], (DEPTH, D_MODEL, N_EXPERTS), jnp.float32) * D_MODEL ** -0.5,
        'b_expert': 0.01 * nrm(ks[23], (DEPTH, N_EXPERTS), jnp.float32),
        'w1': nrm(ks[24], (DEPTH, N_EXPERTS, D_MODEL, D_EXPERT), jnp.float32) * D_MODEL ** -0.5,
        'w3': nrm(ks[25], (DEPTH, N_EXPERTS, D_MODEL, D_EXPERT), jnp.float32) * D_MODEL ** -0.5,
        'w2': nrm(ks[26], (DEPTH, N_EXPERTS, D_EXPERT, D_MODEL), jnp.float32) * D_EXPERT ** -0.5 * ((2 * DEPTH) ** -0.5),
    }

def first_block(x, positions, attn_norm, w_in, m_conv_w, m_conv_b, m_gate_bias, a_q_norm, a_kv_norm,
              a_w_uq, a_w_ukv, a_q_head_norm, a_k_head_norm, c_v_norm, c_w_s, c_b_s, mix_out_norm,
              w_out, ffn_norm, w_group, b_group, w_expert, b_expert, w1, w3, w2):
    B, S, _ = x.shape
    cos, sin = rope_tables(positions)
    for l in range(DEPTH):
        h = rms_norm(x, attn_norm[l])
        proj = h @ w_in[l]
        mq, mk, mv, mo, mi, mf, cq, ckv, krope, cu, cv = split_cols(proj, IN_SIZES)
        qk = jax.nn.silu(causal_depthwise_conv(jnp.concatenate([mq, mk], axis=-1), m_conv_w[l], m_conv_b[l]))
        mq, mk = qk[..., :M_WIDTH], qk[..., M_WIDTH:]
        gb = m_gate_bias[l]
        hm = mlstm_chunkwise(mq.reshape(B, S, M_HEADS, M_HEAD_DIM),
                             mk.reshape(B, S, M_HEADS, M_HEAD_DIM),
                             mv.reshape(B, S, M_HEADS, M_HEAD_DIM),
                             mi + gb[:M_HEADS], mf + gb[M_HEADS:])
        hm = jax.nn.sigmoid(mo) * hm.reshape(B, S, M_WIDTH)
        ha = mla_mixer(cq, ckv, krope, cos, sin, a_q_norm[l], a_kv_norm[l], a_w_uq[l], a_w_ukv[l],
                       a_q_head_norm[l], a_k_head_norm[l])
        hc = chunk_spatial_gating(jax.nn.gelu(cu), jax.nn.gelu(cv), c_v_norm[l], c_w_s[l], c_b_s[l])
        g = mix_out_norm[l]
        y = jnp.concatenate([head_rms_norm(hm, g[:M_WIDTH], M_HEADS),
                             head_rms_norm(ha, g[M_WIDTH:M_WIDTH + A_WIDTH], A_HEADS),
                             head_rms_norm(hc, g[M_WIDTH + A_WIDTH:], C_GROUPS)], axis=-1)
        x = x + y @ w_out[l]
        x = x + hier_moe(rms_norm(x, ffn_norm[l]), w_group[l], b_group[l], w_expert[l], b_expert[l],
                         w1[l], w3[l], w2[l])
    return x


N_MEM = 256
HEAD_DIM = 64
ROT_DIM = HEAD_DIM // 4
ROPE_THETA_2 = 500000.0
NEG_INF = -1e30
N_MIXERS = 3

A_HEADS_2 = D_MODEL // HEAD_DIM
A_WIDTH_2 = A_HEADS_2 * HEAD_DIM
A_PATTERNS = ((128, 1), (512, 4), (2048, 16))
A_BLOCK = 64

B_HEADS = D_MODEL // (2 * HEAD_DIM)
B_WIDTH = B_HEADS * 2 * HEAD_DIM
B_QBLOCK = 128

C_HEADS = D_MODEL // HEAD_DIM
C_KV_HEADS = max(1, C_HEADS // 8)
C_GROUP = C_HEADS // C_KV_HEADS
C_Q_WIDTH = C_HEADS * HEAD_DIM
C_KV_WIDTH = C_KV_HEADS * HEAD_DIM
C_RADIUS = 128
C_BLOCK = 128

X_HEADS = 4
X_HEAD_DIM = D_MODEL // X_HEADS

_FF_RAW = -(-8 * D_MODEL // 3)
D_FF = -(-_FF_RAW // 256) * 256

N_A = len(range(0, DEPTH, N_MIXERS))
N_B = len(range(1, DEPTH, N_MIXERS))
N_C = len(range(2, DEPTH, N_MIXERS))


def rms_norm_2(x, g):
    xf = x.astype(jnp.float32)
    y = xf * lax.rsqrt(jnp.mean(xf * xf, axis=-1, keepdims=True) + EPS)
    return (y * g.astype(jnp.float32)).astype(x.dtype)

def split_heads(t, n):
    b, s, _ = t.shape
    return t.reshape(b, s, n, -1).transpose(0, 2, 1, 3)

def merge_heads(t):
    b, n, s, d = t.shape
    return t.transpose(0, 2, 1, 3).reshape(b, s, n * d)

def rope_tables_2(positions):
    inv_freq = ROPE_THETA_2 ** (-jnp.arange(0, ROT_DIM, 2, dtype=jnp.float32) / ROT_DIM)
    ang = positions.astype(jnp.float32)[..., None] * inv_freq
    return jnp.cos(ang), jnp.sin(ang)

def apply_partial_rope(t, cos, sin):
    shape = (cos.shape[0],) + (1,) * (t.ndim - 3) + cos.shape[1:]
    c = cos.reshape(shape).astype(t.dtype)
    s = sin.reshape(shape).astype(t.dtype)
    half = ROT_DIM // 2
    t1, t2, rest = t[..., :half], t[..., half:ROT_DIM], t[..., ROT_DIM:]
    return jnp.concatenate([t1 * c - t2 * s, t2 * c + t1 * s, rest], axis=-1)

def banded_attention(q, k, v, radius, block, sink=None):
    L = q.shape[-2]
    nb = -(-L // block)
    pad = nb * block - L

    def pad_seq(t, lo, hi):
        return jnp.pad(t, [(0, 0)] * (t.ndim - 2) + [(lo, hi), (0, 0)])

    qb = pad_seq(q, 0, pad).reshape(q.shape[:-2] + (nb, block, q.shape[-1]))

    def band(t):
        tp = pad_seq(t, block, block + pad).reshape(t.shape[:-2] + (nb + 2, block, t.shape[-1]))
        return jnp.concatenate([tp[..., :-2, :, :], tp[..., 1:-1, :, :], tp[..., 2:, :, :]], axis=-2)

    kb, vb = band(k), band(v)
    s = jnp.einsum('...gnqd,...nkd->...gnqk', qb, kb,
                   preferred_element_type=jnp.float32) * (q.shape[-1] ** -0.5)
    qpos = jnp.arange(nb * block).reshape(nb, block, 1)
    kpos = (jnp.arange(nb)[:, None, None] - 1) * block + jnp.arange(3 * block)[None, None, :]
    valid = (jnp.abs(kpos - qpos) <= radius) & (kpos >= 0) & (kpos < L)
    s = jnp.where(valid, s, NEG_INF)
    m = jnp.max(s, axis=-1, keepdims=True)
    if sink is not None:
        sink = sink.astype(jnp.float32)
        m = jnp.maximum(m, sink)
    p = jnp.exp(s - m)
    denom = jnp.sum(p, axis=-1, keepdims=True)
    if sink is not None:
        denom = denom + jnp.exp(sink - m)
    o = jnp.einsum('...gnqk,...nkd->...gnqd', p.astype(v.dtype), vb,
                   preferred_element_type=jnp.float32) / denom
    lse = (m + jnp.log(denom))[..., 0]
    o = o.reshape(o.shape[:-3] + (nb * block, o.shape[-1]))[..., :L, :]
    lse = lse.reshape(lse.shape[:-2] + (nb * block,))[..., :L]
    return o, lse

def dilated_attention_mixer(u, w_in, w_out, cos, sin):
    b, s_len, _ = u.shape
    q, k, v = jnp.split(u @ w_in, 3, axis=-1)
    q = apply_partial_rope(split_heads(q, A_HEADS_2), cos, sin)
    k = apply_partial_rope(split_heads(k, A_HEADS_2), cos, sin)
    v = split_heads(v, A_HEADS_2)
    outs, lses = [], []
    for window, dil in A_PATTERNS:
        radius = window // (2 * dil)

        def by_residue(t):
            return t.reshape(b, A_HEADS_2, s_len // dil, dil, HEAD_DIM).swapaxes(2, 3)

        o, lse = banded_attention(by_residue(q)[..., None, :, :], by_residue(k), by_residue(v),
                                  radius, A_BLOCK)
        outs.append(o[..., 0, :, :].swapaxes(2, 3).reshape(b, A_HEADS_2, s_len, HEAD_DIM))
        lses.append(lse[..., 0, :].swapaxes(2, 3).reshape(b, A_HEADS_2, s_len))
    w = jax.nn.softmax(jnp.stack(lses), axis=0)
    o = jnp.einsum('pbhs,pbhsd->bhsd', w, jnp.stack(outs))
    return merge_heads(o).astype(u.dtype) @ w_out

def differential_attention_mixer(u, w_in, w_out, lam_q1, lam_k1, lam_q2, lam_k2, sub_g,
                                 cos, sin, layer_idx):
    b, s_len, _ = u.shape
    q, k, v = jnp.split(u @ w_in, 3, axis=-1)

    def qk_heads(t):
        return t.reshape(b, s_len, B_HEADS, 2, HEAD_DIM).transpose(0, 2, 3, 1, 4)

    q = apply_partial_rope(qk_heads(q), cos, sin)
    k = apply_partial_rope(qk_heads(k), cos, sin)
    v = split_heads(v, B_HEADS)
    lam_init = 0.8 - 0.6 * math.exp(-0.3 * layer_idx)
    f32 = jnp.float32
    lam = (jnp.exp(jnp.sum(lam_q1.astype(f32) * lam_k1.astype(f32)))
           - jnp.exp(jnp.sum(lam_q2.astype(f32) * lam_k2.astype(f32))) + lam_init)
    nqb = s_len // B_QBLOCK
    qb = q.reshape(b, B_HEADS, 2, nqb, B_QBLOCK, HEAD_DIM).transpose(3, 0, 1, 2, 4, 5)
    scale = HEAD_DIM ** -0.5

    def one_block(qblk):
        sc = jnp.einsum('bhcqd,bhckd->bhcqk', qblk, k, preferred_element_type=f32) * scale
        p = jax.nn.softmax(sc, axis=-1)
        a = p[:, :, 0] - lam * p[:, :, 1]
        return jnp.einsum('bhqk,bhkd->bhqd', a.astype(v.dtype), v, preferred_element_type=f32)

    o = lax.map(one_block, qb)
    o = o.transpose(1, 2, 0, 3, 4).reshape(b, B_HEADS, s_len, 2 * HEAD_DIM)
    o = rms_norm_2(o, sub_g) * (1.0 - lam_init)
    return merge_heads(o).astype(u.dtype) @ w_out

def windowed_gqa_sink_mixer(u, w_in, w_out, sink, cos, sin):
    b, s_len, _ = u.shape
    qkv = u @ w_in
    q = qkv[..., :C_Q_WIDTH]
    k = qkv[..., C_Q_WIDTH:C_Q_WIDTH + C_KV_WIDTH]
    v = qkv[..., C_Q_WIDTH + C_KV_WIDTH:]
    q = apply_partial_rope(split_heads(q, C_HEADS), cos, sin)
    k = apply_partial_rope(split_heads(k, C_KV_HEADS), cos, sin)
    v = split_heads(v, C_KV_HEADS)
    q = q.reshape(b, C_KV_HEADS, C_GROUP, s_len, HEAD_DIM)
    o, _ = banded_attention(q, k, v, C_RADIUS, C_BLOCK,
                            sink=sink.reshape(1, C_KV_HEADS, C_GROUP, 1, 1, 1))
    o = o.reshape(b, C_HEADS, s_len, HEAD_DIM)
    return merge_heads(o).astype(u.dtype) @ w_out

def memory_cross_attention(u, mem_n, wq, wkv, wo):
    q = split_heads(u @ wq, X_HEADS)
    k, v = jnp.split(mem_n @ wkv, 2, axis=-1)
    k = split_heads(k, X_HEADS)
    v = split_heads(v, X_HEADS)
    s = jnp.einsum('bhqd,bhkd->bhqk', q, k,
                   preferred_element_type=jnp.float32) * (X_HEAD_DIM ** -0.5)
    p = jax.nn.softmax(s, axis=-1)
    o = jnp.einsum('bhqk,bhkd->bhqd', p.astype(v.dtype), v)
    return merge_heads(o) @ wo

def swiglu_ffn(u, w_gate_up, w_down):
    g, up = jnp.split(u @ w_gate_up, 2, axis=-1)
    return (jax.nn.silu(g) * up) @ w_down

def second_inputs(seed: int = 0) -> dict:
    key = jax.random.key(seed)
    ks = iter(jax.random.split(key, 32))

    def nrm(shape, scale):
        return jax.random.normal(next(ks), shape, jnp.float32) * scale

    def dense(shape):
        return nrm(shape, shape[-2] ** -0.5)

    def gain(shape):
        return 1.0 + nrm(shape, 0.05)

    x = nrm((BATCH, SEQ, D_MODEL), 1.0)
    mem = nrm((BATCH, N_MEM, D_MODEL), 1.0)
    offset = jax.random.randint(next(ks), (BATCH, 1), 0, 4096, dtype=jnp.int32)
    positions = jnp.arange(SEQ, dtype=jnp.int32)[None, :] + offset
    return {
        "x": x, "mem": mem, "positions": positions,
        "mix_pre_g": gain((DEPTH, D_MODEL)), "mix_post_g": gain((DEPTH, D_MODEL)),
        "mem_pre_g": gain((DEPTH, D_MODEL)), "mem_kv_g": gain((DEPTH, D_MODEL)),
        "mem_post_g": gain((DEPTH, D_MODEL)),
        "ffn_pre_g": gain((DEPTH, D_MODEL)), "ffn_post_g": gain((DEPTH, D_MODEL)),
        "a_w_in": dense((N_A, D_MODEL, 3 * A_WIDTH_2)), "a_w_out": dense((N_A, A_WIDTH_2, D_MODEL)),
        "b_w_in": dense((N_B, D_MODEL, 3 * B_WIDTH)), "b_w_out": dense((N_B, B_WIDTH, D_MODEL)),
        "b_lam_q1": nrm((N_B, HEAD_DIM), 0.1), "b_lam_k1": nrm((N_B, HEAD_DIM), 0.1),
        "b_lam_q2": nrm((N_B, HEAD_DIM), 0.1), "b_lam_k2": nrm((N_B, HEAD_DIM), 0.1),
        "b_sub_g": gain((N_B, 2 * HEAD_DIM)),
        "c_w_in": dense((N_C, D_MODEL, C_Q_WIDTH + 2 * C_KV_WIDTH)),
        "c_w_out": dense((N_C, C_Q_WIDTH, D_MODEL)),
        "c_sink": nrm((N_C, C_HEADS), 0.5),
        "x_wq": dense((DEPTH, D_MODEL, D_MODEL)), "x_wkv": dense((DEPTH, D_MODEL, 2 * D_MODEL)),
        "x_wo": dense((DEPTH, D_MODEL, D_MODEL)),
        "w_gate_up": dense((DEPTH, D_MODEL, 2 * D_FF)), "w_down": dense((DEPTH, D_FF, D_MODEL)),
    }

def second_block(x, mem, positions, mix_pre_g, mix_post_g, mem_pre_g, mem_kv_g, mem_post_g,
              ffn_pre_g, ffn_post_g, a_w_in, a_w_out, b_w_in, b_w_out, b_lam_q1, b_lam_k1,
              b_lam_q2, b_lam_k2, b_sub_g, c_w_in, c_w_out, c_sink, x_wq, x_wkv, x_wo,
              w_gate_up, w_down):
    cos, sin = rope_tables_2(positions)
    h = x
    for i in range(DEPTH):
        kind, j = i % N_MIXERS, i // N_MIXERS
        u = rms_norm_2(h, mix_pre_g[i])
        if kind == 0:
            y = dilated_attention_mixer(u, a_w_in[j], a_w_out[j], cos, sin)
        elif kind == 1:
            y = differential_attention_mixer(u, b_w_in[j], b_w_out[j], b_lam_q1[j], b_lam_k1[j],
                                             b_lam_q2[j], b_lam_k2[j], b_sub_g[j], cos, sin, i)
        else:
            y = windowed_gqa_sink_mixer(u, c_w_in[j], c_w_out[j], c_sink[j], cos, sin)
        h = h + rms_norm_2(y, mix_post_g[i])
        u = rms_norm_2(h, mem_pre_g[i])
        y = memory_cross_attention(u, rms_norm_2(mem, mem_kv_g[i]), x_wq[i], x_wkv[i], x_wo[i])
        h = h + rms_norm_2(y, mem_post_g[i])
        u = rms_norm_2(h, ffn_pre_g[i])
        y = swiglu_ffn(u, w_gate_up[i], w_down[i])
        h = h + rms_norm_2(y, ffn_post_g[i])
    return h


def setup_inputs(seed=0):
    out = dict(first_inputs(seed))
    for name, value in second_inputs(seed + 1).items():
        if name != "x":
            out[name + "_2"] = value
    return out


def reference(
    x, positions, attn_norm, w_in, m_conv_w, m_conv_b, m_gate_bias, a_q_norm, a_kv_norm, a_w_uq,
    a_w_ukv, a_q_head_norm, a_k_head_norm, c_v_norm, c_w_s, c_b_s, mix_out_norm, w_out,
    ffn_norm, w_group, b_group, w_expert, b_expert, w1, w3, w2, mem_2, positions_2, mix_pre_g_2,
    mix_post_g_2, mem_pre_g_2, mem_kv_g_2, mem_post_g_2, ffn_pre_g_2, ffn_post_g_2, a_w_in_2,
    a_w_out_2, b_w_in_2, b_w_out_2, b_lam_q1_2, b_lam_k1_2, b_lam_q2_2, b_lam_k2_2, b_sub_g_2,
    c_w_in_2, c_w_out_2, c_sink_2, x_wq_2, x_wkv_2, x_wo_2, w_gate_up_2, w_down_2,
):
    x = first_block(
        x, positions, attn_norm, w_in, m_conv_w, m_conv_b, m_gate_bias, a_q_norm, a_kv_norm,
        a_w_uq, a_w_ukv, a_q_head_norm, a_k_head_norm, c_v_norm, c_w_s, c_b_s, mix_out_norm,
        w_out, ffn_norm, w_group, b_group, w_expert, b_expert, w1, w3, w2,
    )
    return second_block(
        x, mem_2, positions_2, mix_pre_g_2, mix_post_g_2, mem_pre_g_2, mem_kv_g_2, mem_post_g_2,
        ffn_pre_g_2, ffn_post_g_2, a_w_in_2, a_w_out_2, b_w_in_2, b_w_out_2, b_lam_q1_2,
        b_lam_k1_2, b_lam_q2_2, b_lam_k2_2, b_sub_g_2, c_w_in_2, c_w_out_2, c_sink_2, x_wq_2,
        x_wkv_2, x_wo_2, w_gate_up_2, w_down_2,
    )


_drawn_inputs = setup_inputs


def setup_inputs(seed=0):
    import zlib

    import numpy as np

    out = dict(_drawn_inputs(seed))
    spreads = {}
    factors = {'m_conv_b': 3.65,
     'a_q_norm': 4.406,
     'a_kv_norm': 2.764,
     'a_q_head_norm': 5.742,
     'a_k_head_norm': 4.276,
     'c_v_norm': 8.0,
     'c_b_s': 2.912,
     'ffn_norm': 3.095,
     'b_group': 8.0,
     'b_expert': 5.574,
     'b_lam_q1_2': 64.0,
     'b_lam_k1_2': 64.0,
     'b_lam_q2_2': 200.0,
     'b_lam_k2_2': 8.0,
     'mem_pre_g_2': 3.049,
     'ffn_post_g_2': 3.163,
     'b_sub_g_2': 19.262}
    for name, (base, spread) in spreads.items():
        noise = np.random.default_rng([zlib.crc32(name.encode()), seed]).standard_normal(out[name].shape)
        drawn = base * np.exp(spread * noise) if base else spread * noise
        out[name] = jnp.asarray(drawn.astype(out[name].dtype))
    for name, factor in factors.items():
        out[name] = (out[name] * factor).astype(out[name].dtype)
    return out
```

```python
import concourse.bass as bass
from concourse import mybir
from contextlib import ExitStack

P = 128
D = 1024
S = 512
TT = S // P
KC = D // P
LAYERS = 2
BANK = 512
EPS = 1e-6

M_HEADS, M_DIM = 4, 96
M_WIDTH = M_HEADS * M_DIM
M_PAD = M_DIM + 1
CONV = 4
QK_TILES = 2 * M_HEADS
A_HEADS, A_NOPE, A_ROPE, A_V = 6, 64, 32, 64
A_QK = A_NOPE + A_ROPE
A_Q_RANK, A_KV_RANK = 256, 128
A_KV = A_NOPE + A_V
C_GROUPS, C_DIM = 4, 64
C_WIDTH = C_GROUPS * C_DIM
OFF_V = 0
OFF_O = OFF_V + M_HEADS * M_PAD
OFF_CQ = OFF_O + M_WIDTH
OFF_CKV = OFF_CQ + A_Q_RANK
OFF_KR = OFF_CKV + A_KV_RANK
OFF_CU = OFF_KR + A_ROPE
OFF_CV = OFF_CU + C_WIDTH
TOK_W = OFF_CV + C_WIDTH

N_GROUPS, PER_GROUP = 4, 8
N_EXP = N_GROUPS * PER_GROUP
D_EXP = 256
N_BLK = (2 * S + N_EXP * (P - 1)) // P
E_SLOTS = 3
E_STEPS = N_BLK // E_SLOTS
TABLE_W = N_BLK + 1
assert E_STEPS * E_SLOTS == N_BLK

N_MEM, MT = 256, 2
HD = 64
ROT = 16
X_HEADS, X_DIM = 4, 256
FF = 2816
FC = FF // P
LAM_INIT = 0.8 - 0.6 * 2.718281828459045 ** (-0.3)


def layout(fields):
    at, out = 0, {}
    for name, width in fields:
        out[name] = (at, width)
        at += width
    return out, at


CONSTS, CONST_W = layout([
    ("ident", P), ("ones", P), ("before", P), ("upto", P), ("causal", S), ("dilated", TT * S),
    ("iota", N_EXP), ("blocks", N_BLK), ("pick", M_HEADS * P), ("freq1", A_ROPE // 2), ("freq2", ROT // 2)])
PAR1, PAR1_W = layout([
    ("attn_g", KC), ("conv_w", QK_TILES * CONV), ("conv_b", QK_TILES), ("gate_b", 2), ("cq_g", 2), ("ckv_g", 1),
    ("qh_g", A_QK), ("kh_g", A_QK), ("cv_g", C_WIDTH), ("w_s", C_GROUPS * P), ("b_s", C_GROUPS), ("out_g", KC),
    ("ffn_g", KC), ("group_b", N_GROUPS), ("exp_b", N_EXP), ("w_gate", KC * 2 * M_HEADS),
    ("w_uq", 2 * A_HEADS * A_QK), ("w_ukv", A_HEADS * A_KV), ("w_route", KC * (N_GROUPS + N_EXP))])
PAR2, PAR2_W = layout([
    ("mix_g", KC), ("mem_g", KC), ("memkv_g", KC), ("ffn_g", KC), ("mix_post", D), ("mem_post", D), ("ffn_post", D),
    ("sub_g", 1), ("lam", 4 * HD)])
PAR_W = max(PAR1_W, PAR2_W)


def program(nc, a):
    f32, i32 = mybir.dt.float32, mybir.dt.int32
    ACT, ALU, AX = mybir.ActivationFunctionType, mybir.AluOpType, mybir.AxisListType
    ds = bass.ds
    V, A, G, T = nc.vector, nc.scalar, nc.gpsimd, nc.tensor
    ctx = ExitStack()
    with ctx:
        def sb(name, width, dt=f32):
            return ctx.enter_context(nc.sbuf_tensor(name, [P, width], dt))

        def sem(name):
            return ctx.enter_context(nc.semaphore(name))

        x_all = sb("x_res", TT * D)
        feat = sb("feat", KC * S)
        RING = 4096
        ring = sb("ring", 2 * RING)
        par = [sb(f"par{i}", PAR_W) for i in range(2)]
        cst = sb("cst", CONST_W)
        big = sb("big", 12288)
        tmp = sb("tmp", 11264)
        rope = sb("rope", 2 * TT * (A_ROPE // 2 + ROT // 2))
        stat = sb("stat", 256)
        rows = sb("rows", 3 * S)
        R_IDX = 4 * TT + TABLE_W + N_BLK + TT
        route_i = sb("route_i", R_IDX + E_SLOTS + 1, i32)
        ps = ctx.enter_context(nc.psum_tensor("ps", [P, 8, BANK], f32))

        x = x_all[:, :].rearrange("p (t d) -> p t d", t=TT)
        featv = feat[:, :].rearrange("p (c s) -> p c s", c=KC)

        def c_(name):
            o, w = CONSTS[name]
            return cst[:, o:o + w]

        def p1(l, name):
            o, w = PAR1[name]
            return par[l][:, o:o + w]

        def p2(l, name):
            o, w = PAR2[name]
            return par[l][:, o:o + w]

        def view(buf, at, *shape):
            n = 1
            for s in shape:
                n *= s
            v = buf[:, at:at + n]
            if len(shape) == 1:
                return v
            names = "abcd"[:len(shape)]
            left = " ".join(names)
            return v.rearrange(f"p ({left}) -> p {left}", **{k: s for k, s in zip(names, shape)})

        ident = c_("ident")
        cos1, sin1 = view(rope, 0, TT, 16), view(rope, 64, TT, 16)
        cos2, sin2 = view(rope, 128, TT, 8), view(rope, 160, TT, 8)

        done = {e: sem(f"{e}_phase_done") for e in ("pe", "act", "dve", "pool")}
        const_loaded, par_loaded = sem("const_loaded"), [sem("par0_loaded"), sem("par1_loaded")]
        x_loaded, pos_loaded, mem_loaded = sem("x_loaded"), sem("pos_loaded"), sem("mem_loaded")
        pads_zeroed = sem("pads_zeroed")
        ids_loaded, par2_loaded = sem("ids_loaded"), sem("par2_loaded")
        w_loaded = [sem("w_slot0_loaded"), sem("w_slot1_loaded")]
        w_used = sem("w_used")
        bank_full = sem("bank_full")
        bank_read_dve, bank_read_act = sem("bank_read_dve"), sem("bank_read_act")
        staged, turned, qT_ready, kT_ready = sem("staged"), sem("turned"), sem("qT_ready"), sem("kT_ready")
        scores_ready, max_ready, probs_ready = sem("scores_ready"), sem("max_ready"), sem("probs_ready")
        mixed_ready, probsT_full, probsT_ready = sem("mixed_ready"), sem("probsT_full"), sem("probsT_ready")
        out_full, out_read = sem("out_full"), sem("out_read")
        decay_in, decay_ready = sem("decay_in"), sem("decay_ready")
        normed_out, table_zeroed, table_filled, table_read = (
            sem("normed_out"), sem("table_zeroed"), sem("table_filled"), sem("table_read"))
        e_loaded = [sem(f"e{s}_loaded") for s in range(E_SLOTS)]
        e_rows = [sem(f"e{s}_rows") for s in range(E_SLOTS)]
        e_turned = [sem(f"e{s}_turned") for s in range(E_SLOTS)]
        e_rowsT = [sem(f"e{s}_rowsT") for s in range(E_SLOTS)]
        e_up = [sem(f"e{s}_up") for s in range(E_SLOTS)]
        e_silu = [sem(f"e{s}_silu") for s in range(E_SLOTS)]
        e_hidden = [sem(f"e{s}_hidden") for s in range(E_SLOTS)]
        e_hturned = [sem(f"e{s}_hturned") for s in range(E_SLOTS)]
        e_hiddenT = [sem(f"e{s}_hiddenT") for s in range(E_SLOTS)]
        e_down = [sem(f"e{s}_down") for s in range(E_SLOTS)]
        e_copied = [sem(f"e{s}_copied") for s in range(E_SLOTS)]
        e_stored = [sem(f"e{s}_stored") for s in range(E_SLOTS)]
        pair_loaded = [sem("pair0_loaded"), sem("pair1_loaded")]
        out_stored = sem("out_stored")

        count = {}

        def take(engine, what, n=1):
            at = count.get((engine, what), 0)
            count[(engine, what)] = at + n
            return at

        def phase(name, eng):
            n = take(name, "phase") + 1
            eng.drain().then_inc(done[name], 1)
            for other, s in done.items():
                if other != name:
                    eng.wait_ge(s, n)

        def bcast(ap, shape):
            return ap.to_broadcast(shape)

        def pe_banks(pe, jobs):
            q0 = take("pe", "bank", len(jobs))
            for i, job in enumerate(jobs):
                q = q0 + i
                if q >= 8:
                    pe.wait_ge(bank_read_act if q % 2 else bank_read_dve, (q - 8) // 2 + 1)
                last = None
                for m in job(ps[:, q % 8, :]):
                    last = m
                last.then_inc(bank_full, 1)

        def read_banks(name, eng, reads):
            q0 = take(name, "bank", len(reads))
            for i, read in enumerate(reads):
                q = q0 + i
                if q % 2 == (name == "act"):
                    eng.wait_ge(bank_full, q + 1)
                    read(ps[:, q % 8, :]).then_inc(bank_read_act if name == "act" else bank_read_dve, 1)

        def copier(name, dst, n, gain=None, parts=P):
            def read(bank):
                src = bank[0:parts, 0:n]
                if name == "act":
                    return A.activation(dst, src, ACT.Copy, scale=1.0 if gain is None else gain)
                if gain is None:
                    return V.tensor_copy(dst, src)
                return V.tensor_scalar(dst, src, gain, None, ALU.mult)
            return read

        def turn_jobs(src, chunks, tiles=TT, width=P):
            def job(c):
                def run(bank):
                    for t in range(tiles):
                        yield T.transpose(bank[0:width, t * P:(t + 1) * P],
                                          src[:, t, c * width:(c + 1) * width], ident)
                return run
            return [job(c) for c in range(chunks)]

        def turn(name, eng, src, dst, chunks, gain=None, tiles=TT):
            if name == "pe":
                pe_banks(eng, turn_jobs(src, chunks, tiles))
            else:
                read_banks(name, eng, [copier(name, dst[:, c, :], tiles * P,
                                              None if gain is None else gain[:, c:c + 1]) for c in range(chunks)])
            phase(name, eng)

        def ring_slot(n, kc, width):
            return view(ring, (n % 2) * RING, kc, width)

        def project(name, eng, lhs, widths, dst, tiles=TT, kc=KC, beside=()):
            col = 0
            beside = list(beside)
            for width in widths:
                n = take(name, "ring")
                if name == "pe":
                    w = ring_slot(n, kc, width)
                    eng.wait_ge(w_loaded[n % 2], 16 * (n // 2 + 1))

                    def job(t, w=w, width=width):
                        def run(bank):
                            for k in range(kc):
                                yield T.matmul(bank[:, 0:width], lhs[:, k, t * P:(t + 1) * P], w[:, k, :],
                                               start=k == 0, stop=k == kc - 1)
                        return run
                    pe_banks(eng, [job(t) for t in range(tiles)])
                    eng.drain().then_inc(w_used, 1)
                else:
                    read_banks(name, eng, [copier(name, dst[:, t, col:col + width], width) for t in range(tiles)])
                    if beside:
                        beside.pop(0)()
                col += width
            phase(name, eng)

        def rsqrt(pool, v, size):
            half = stat[:, 255:256]
            G.tensor_scalar(v, v, 1.0 / size, EPS, ALU.mult, ALU.add)
            pool.drain()
            G.tensor_tensor(out=v, in0=v, in1=bcast(half, [P, v.shape[1]]), op=ALU.pow)

        def norm(name, eng, src, xn, dst, gain, tiles=TT):
            ss = stat[:, 0:tiles]
            for t in range(tiles):
                if name == "act" and t % 2 == 0:
                    A.activation(xn[:, t, :], src[:, t, :], ACT.Square, accum_out=ss[:, t:t + 1])
                if name == "dve" and t % 2 == 1:
                    V.tensor_tensor_reduce(out=xn[:, t, :], in0=src[:, t, :], in1=src[:, t, :], scale=1.0, scalar=0.0,
                                           op0=ALU.mult, op1=ALU.add, accum_out=ss[:, t:t + 1])
            phase(name, eng)
            if name == "pool":
                rsqrt(eng, ss, D)
            phase(name, eng)
            for t in range(tiles):
                if name == "act" and t % 4 == 0:
                    A.activation(xn[:, t, :], src[:, t, :], ACT.Copy, scale=ss[:, t:t + 1])
                if name == "dve" and t % 4:
                    V.tensor_scalar(xn[:, t, :], src[:, t, :], ss[:, t:t + 1], None, ALU.mult)
            phase(name, eng)
            turn(name, eng, xn, dst, KC, gain, tiles)

        def attention(name, eng, cfg):
            steps, units = cfg["steps"], cfg["units"]
            n_u = len(units)
            c0, b0 = take(name, "att_step", steps), take(name, "att_unit", steps * n_u)
            st = tmp
            at = [cfg.get("at", 0)]

            def room(*shape):
                v = view(st, at[0], *shape)
                for_all = 1
                for s in shape:
                    for_all *= s
                at[0] += for_all
                return v

            qd, parts = cfg["qd"], cfg["parts"]
            nq = qd // parts
            kt = cfg["key_tiles"]
            qs, ks = room(TT, qd), room(kt, qd)
            qT, kT = room(nq, S), room(nq, kt * P)
            score = [room(S), room(S)]
            prob = [room(S), room(S)]
            probT = [room(TT, P), room(TT, P)]
            nmax, rsum, rinvs = stat[:, 16:18], stat[:, 20:24], stat[:, 24:28]
            scale, mask = cfg["scale"], cfg["mask"]
            k_bank = 7 if nq == 1 else 5

            ahead = nq == 1

            def stage_heads(c):
                if name == "dve":
                    V.tensor_copy(qs, cfg["q"](c))
                    V.tensor_copy(ks, cfg["k"](c)).then_inc(staged, 1)

            def turn_heads(c):
                n = c0 + c + 1
                if name == "dve":
                    eng.wait_ge(turned, n)
                    V.tensor_copy(kT[0:parts], ps[0:parts, k_bank, 0:nq * kt * P]
                                  .rearrange("p (a s) -> p a s", a=nq)).then_inc(kT_ready, 1)
                if name == "pe":
                    eng.wait_ge(staged, n)
                    for j in range(nq):
                        for t in range(TT):
                            T.transpose(ps[0:parts, 6 + j, t * P:(t + 1) * P], qs[:, t, j * parts:(j + 1) * parts], ident)
                    for j in range(nq):
                        for t in range(kt):
                            o = (j * kt + t) * P
                            last = T.transpose(ps[0:parts, k_bank, o:o + P], ks[:, t, j * parts:(j + 1) * parts], ident)
                    last.then_inc(turned, 1)
                if name == "act":
                    eng.wait_ge(turned, n)
                    A.activation(qT[0:parts], ps[0:parts, 6:6 + nq, :], ACT.Copy).then_inc(qT_ready, 1)

            def body(c, more=True):
                b, n = b0 + c * n_u, c0 + c + 1
                if not ahead:
                    stage_heads(c)
                    turn_heads(c)
                if name == "pe":
                    eng.wait_ge(qT_ready, n)
                    eng.wait_ge(kT_ready, n)

                def scores(u):
                    lo, hi, t, width = units[u][:4]
                    if u >= 2:
                        eng.wait_ge(max_ready if mask is not None else probs_ready, b + u - 1)
                    for j in range(nq):
                        m = T.matmul(ps[:, u % 2, 0:width], qT[lo:hi, j, t * P:(t + 1) * P], kT[lo:hi, j, 0:width],
                                     start=j == 0, stop=j == nq - 1)
                    m.then_inc(scores_ready, 1)

                def turn_probs(u):
                    width = units[u][3]
                    eng.wait_ge(probs_ready, b + u + 1)
                    if u >= 2:
                        eng.wait_ge(probsT_ready, b + u - 1)
                    for s in range(width // P):
                        m = T.transpose(ps[:, 2 + u % 2, s * P:(s + 1) * P], prob[u % 2][:, s * P:(s + 1) * P], ident)
                    m.then_inc(probsT_full, 1)

                def output(u):
                    width, sub = units[u][3], units[u][4]
                    eng.wait_ge(probsT_ready, b + u + 1)
                    if u >= 2:
                        eng.wait_ge(out_read, b + u - 1)
                    ns = width // P
                    for s in range(ns):
                        m = T.matmul(ps[:, 4 + u % 2, 0:cfg["vd"]], probT[u % 2][:, s, :], cfg["v"](c, s, sub),
                                     start=s == 0, stop=s == ns - 1)
                    m.then_inc(out_full, 1)

                def maximum(u):
                    t, width = units[u][2:4]
                    eng.wait_ge(scores_ready, b + u + 1)
                    if u >= 2:
                        eng.wait_ge(probs_ready, b + u - 1)
                    nm = nmax[:, u % 2:u % 2 + 1]
                    if mask is not None:
                        V.scalar_tensor_tensor(out=score[u % 2][:, 0:width], in0=ps[:, u % 2, 0:width], scalar=scale,
                                               in1=mask(t, width), op0=ALU.mult, op1=ALU.add)
                        eng.drain()
                        V.tensor_reduce(nm, score[u % 2][:, 0:width], AX.X, ALU.max, negate=True).then_inc(max_ready, 1)
                    else:
                        V.tensor_reduce(nm, ps[:, u % 2, 0:width], AX.X, ALU.max, negate=True)
                        eng.drain()
                        V.tensor_scalar(nm, nm, scale, None, ALU.mult).then_inc(max_ready, 1)

                def final(u):
                    t, sub = units[u][2], units[u][4]
                    rinv = rinvs[:, u % 4:u % 4 + 1]
                    V.reciprocal(rinv, rsum[:, u % 4:u % 4 + 1])
                    eng.drain()
                    eng.wait_ge(out_full, b + u + 1)
                    V.tensor_scalar(cfg["o"](c, t, sub), ps[:, 4 + u % 2, 0:cfg["vd"]], rinv, None,
                                    ALU.mult).then_inc(out_read, 1)

                def expo(u):
                    width = units[u][3]
                    eng.wait_ge(max_ready, b + u + 1)
                    if u >= 2:
                        eng.wait_ge(probsT_full, b + u - 1)
                    src = ps[:, u % 2, 0:width] if mask is None else score[u % 2][:, 0:width]
                    A.activation(prob[u % 2][:, 0:width], src, ACT.Exp, bias=nmax[:, u % 2:u % 2 + 1],
                                 scale=scale if mask is None else 1.0,
                                 accum_out=rsum[:, u % 4:u % 4 + 1]).then_inc(probs_ready, 1)

                def copyT(u):
                    width = units[u][3]
                    eng.wait_ge(probsT_full, b + u + 1)
                    if u >= 2:
                        eng.wait_ge(out_full, b + u - 1)
                    A.activation(probT[u % 2][:, 0:width // P, :], ps[:, 2 + u % 2, 0:width]
                                 .rearrange("p (a s) -> p a s", s=P), ACT.Copy).then_inc(probsT_ready, 1)

                stages = {"pe": (scores, turn_probs, output), "dve": (maximum, None, final),
                          "act": (expo, copyT, None)}.get(name)
                for u in range(n_u + 2):
                    for lag, stage in enumerate(stages):
                        if stage and 0 <= u - lag < n_u:
                            stage(u - lag)
                        if lag == 0 and u == n_u - 1 and ahead and more and name == "pe":
                            turn_heads(c + 1)
                    if ahead and more and u == 1:
                        stage_heads(c + 1)
                    if ahead and more and u == n_u - 1 and name != "pe":
                        turn_heads(c + 1)

            if name in ("pe", "act", "dve"):
                if ahead:
                    stage_heads(0)
                    turn_heads(0)
                    with eng.Fori(0, steps - 1) as c:
                        body(c)
                    body(steps - 1, more=False)
                else:
                    with eng.Fori(0, steps) as c:
                        body(c)
            phase(name, eng)

        proj = view(big, 0, TT, TOK_W)
        q_lat = view(big, TT * TOK_W, TT, A_HEADS * A_QK)
        kv_lat = view(big, TT * TOK_W + TT * A_HEADS * A_QK, TT, A_HEADS * A_KV)
        mix = view(tmp, 7168, TT, D)
        qk_pad = view(tmp, 0, QK_TILES, S + CONV - 1)
        conv_acc = view(tmp, QK_TILES * (S + CONV - 1), QK_TILES, S)
        qk_conv = view(feat, 0, QK_TILES, S)

        def in_projection(name, eng, l):
            if name == "pool":
                G.memset(qk_pad[:, :, 0:CONV - 1], 0.0).then_inc(pads_zeroed, 1)
            for half in range(2):
                n = take(name, "ring")
                if name == "pe":
                    w = ring_slot(n, KC, M_WIDTH)
                    eng.wait_ge(w_loaded[n % 2], 16 * (n // 2 + 1))

                    def job(h, w=w):
                        def run(bank):
                            for k in range(KC):
                                yield T.matmul(bank[0:M_DIM, :], w[:, k, h * M_DIM:(h + 1) * M_DIM], featv[:, k, :],
                                               start=k == 0, stop=k == KC - 1)
                        return run
                    pe_banks(eng, [job(h) for h in range(M_HEADS)])
                    eng.drain().then_inc(w_used, 1)
                elif name in ("act", "dve"):
                    read_banks(name, eng, [copier(name, qk_pad[0:M_DIM, half * M_HEADS + h, CONV - 1:], S, parts=M_DIM)
                                           for h in range(M_HEADS)])
            w_gate = p1(l, "w_gate").rearrange("p (k g h) -> p k g h", k=KC, g=2)
            if name == "pe":
                def gjob(g):
                    def run(bank):
                        for k in range(KC):
                            yield T.matmul(bank[0:M_HEADS, :], w_gate[:, k, g, :], featv[:, k, :],
                                           start=k == 0, stop=k == KC - 1)
                    return run
                pe_banks(eng, [gjob(0), gjob(1)])
            elif name in ("act", "dve"):
                read_banks(name, eng, [copier(name, rows[0:M_HEADS, g * S:(g + 1) * S], S, parts=M_HEADS)
                                       for g in range(2)])
            beside = ()
            if name == "dve":
                eng.wait_ge(pads_zeroed, l + 1)
                act_reads = count[("dve", "bank")] // 2
                beside = [lambda j=j: conv_tap(eng, l, j, act_reads) for j in range(CONV)]
            project(name, eng, featv, [512, 512, 512, TOK_W - 1536], proj, beside=beside)

        def conv_tap(dve, l, j, act_reads):
            w = p1(l, "conv_w").rearrange("p (t j) -> p t j", t=QK_TILES)
            b = p1(l, "conv_b")
            M = slice(0, M_DIM)
            dve.drain()
            if j == 0:
                dve.wait_ge(bank_read_act, act_reads)
            for t in range(QK_TILES):
                if j == 0:
                    V.tensor_scalar(conv_acc[M, t, :], qk_pad[M, t, 0:S], w[M, t, 0:1], b[M, t:t + 1], ALU.mult, ALU.add)
                else:
                    V.scalar_tensor_tensor(out=conv_acc[M, t, :], in0=qk_pad[M, t, j:j + S], scalar=w[M, t, j:j + 1],
                                           in1=conv_acc[M, t, :], op0=ALU.mult, op1=ALU.add)

        log_i, cum_f, peak = (rows[0:M_HEADS, i * S:(i + 1) * S] for i in range(3))

        m_q, m_k = view(tmp, 0, S), view(tmp, S, S)
        npeak_bc = view(tmp, 2 * S, M_HEADS, S)
        m_decay = [view(tmp, 6 * S, S), view(tmp, 7 * S, S)]
        m_w = view(tmp, 8 * S, TT, S)
        u_col = view(stat, 32, TT, M_HEADS)
        floor_col = view(stat, 48, TT, M_HEADS)

        def conv_and_gates(name, eng, l):
            M = slice(0, M_DIM)
            if name == "dve":
                gb = p1(l, "gate_b")
                H = slice(0, M_HEADS)
                V.tensor_scalar(log_i, log_i, gb[H, 0:1], None, ALU.add)
                V.tensor_scalar(cum_f, cum_f, gb[H, 1:2], None, ALU.add)
                eng.drain()
                V.tensor_scalar(peak, cum_f, -1.0, None, ALU.mult)
                eng.drain()
                V.tensor_tensor(peak, peak, cum_f, ALU.min)
            phase(name, eng)
            if name == "act":
                A.activation(peak, peak, ACT.Exp)
                eng.drain()
                A.activation(peak, peak, ACT.Ln, bias=1.0)
                for t in range(QK_TILES):
                    A.activation(qk_conv[M, t, :], conv_acc[M, t, :], ACT.Silu)
            phase(name, eng)
            if name == "dve":
                V.tensor_scalar(cum_f, cum_f, 0.0, None, ALU.min)
                eng.drain()
                V.tensor_tensor(peak, cum_f, peak, ALU.subtract)
                V.memset(m_q[0:M_HEADS, :], 1.0)
                eng.drain()
                V.tensor_tensor_scan(cum_f, m_q[0:M_HEADS, :], peak, 0.0, ALU.mult, ALU.add)
                eng.drain()
                V.tensor_tensor(log_i, log_i, cum_f, ALU.subtract)
                eng.drain()
                V.tensor_tensor_scan(peak, m_q[0:M_HEADS, :], log_i, 0.0, ALU.mult, ALU.max)
                eng.drain()
                V.tensor_tensor(cum_f, cum_f, peak, ALU.add)
            phase(name, eng)
            pick = c_("pick")
            if name == "pe":
                def pjob(h):
                    def run(bank):
                        yield T.matmul(bank, pick[0:M_HEADS, h * P:(h + 1) * P], peak, start=True, stop=True)
                    return run

                def cjob(src):
                    def run(bank):
                        for t in range(TT):
                            yield T.transpose(bank[:, t * M_HEADS:(t + 1) * M_HEADS], src[:, t * P:(t + 1) * P],
                                              ident[0:M_HEADS, 0:M_HEADS])
                    return run
                pe_banks(eng, [pjob(h) for h in range(M_HEADS)] + [cjob(log_i), cjob(cum_f)])
            elif name in ("act", "dve"):
                reads = []
                for h in range(M_HEADS):
                    def read(bank, h=h):
                        if name == "act":
                            return A.activation(npeak_bc[:, h, :], bank, ACT.Copy, scale=-1.0)
                        return V.tensor_scalar(npeak_bc[:, h, :], bank, -1.0, None, ALU.mult)
                    reads.append(read)
                reads.append(copier(name, stat[:, 32:48], 16))
                reads.append(lambda bank: A.activation(stat[:, 48:64], bank[:, 0:16], ACT.Exp, scale=-1.0))
                read_banks(name, eng, reads)
            phase(name, eng)

        def mlstm(name, eng, l):
            c0 = take(name, "m_step", M_HEADS)
            M = slice(0, M_DIM)
            values = proj[:, :, OFF_V:OFF_V + M_HEADS * M_PAD]
            if name == "dve":
                for h in range(M_HEADS):
                    V.memset(values[:, :, h * M_PAD + M_DIM:(h + 1) * M_PAD], 1.0)
                eng.drain()
            phase(name, eng)

            def body(h):
                n = c0 + h + 1
                b = (c0 + h) * TT

                def weigh(j):
                    width = S - j * P
                    eng.wait_ge(m_scores, b + j + 1)
                    eng.wait_ge(m_decayed, b + j + 1)
                    V.scalar_tensor_tensor(out=m_w[:, j, j * P:S], in0=ps[:, j, 0:width], scalar=float(M_DIM) ** -0.5,
                                           in1=m_decay[j % 2][:, 0:width], op0=ALU.mult, op1=ALU.mult)
                    eng.drain()
                    V.tensor_tensor(m_w[:, j, j * P:(j + 1) * P], m_w[:, j, j * P:(j + 1) * P], c_("upto"),
                                    ALU.mult).then_inc(m_weighed, 1)

                if name == "dve":
                    V.tensor_copy(m_q[M], qk_conv[M, ds(h, 1), :].rearrange("p a s -> p (a s)"))
                    V.tensor_copy(m_k[M], qk_conv[M, ds(h + M_HEADS, 1), :].rearrange("p a s -> p (a s)")).then_inc(m_staged, 1)
                if name == "pe":
                    eng.wait_ge(m_staged, n)
                for j in range(TT):
                    q0, width = j * P, S - j * P
                    if name == "pe":
                        T.matmul(ps[:, j, 0:width], m_k[M, q0:q0 + P], m_q[M, q0:S],
                                 start=True, stop=True).then_inc(m_scores, 1)
                    if name == "dve":
                        if j >= 2:
                            eng.drain()
                        V.tensor_scalar(m_decay[j % 2][:, 0:width], npeak_bc[:, ds(h, 1), q0:S].rearrange("p a s -> p (a s)"),
                                        u_col[:, j, ds(h, 1)], 0.0, ALU.add, ALU.min).then_inc(m_decay_in, 1)
                        if j >= 1:
                            weigh(j - 1)
                    if name == "act":
                        eng.wait_ge(m_decay_in, b + j + 1)
                        d = m_decay[j % 2][:, 0:width]
                        A.activation(d, d, ACT.Exp).then_inc(m_decayed, 1)
                if name == "dve":
                    weigh(TT - 1)
                if name == "pe":
                    eng.wait_ge(m_weighed, b + TT)
                    for t in range(TT):
                        for j in range(t + 1):
                            m = T.matmul(ps[:, 4 + t, 0:M_PAD], m_w[:, j, t * P:(t + 1) * P],
                                         values[:, j, ds(h * M_PAD, M_PAD)], start=j == 0, stop=j == t)
                    m.then_inc(m_out, 1)
                if name == "dve":
                    eng.wait_ge(m_out, n)
                    den, neg = stat[:, 64:68], stat[:, 68:72]
                    V.tensor_copy(den, ps[:, 4:8, M_DIM:M_PAD].rearrange("p t a -> p (t a)"))
                    eng.drain()
                    V.tensor_scalar(neg, den, -1.0, None, ALU.mult)
                    eng.drain()
                    V.tensor_tensor(den, den, neg, ALU.max)
                    eng.drain()
                    V.tensor_tensor(den, den, floor_col[:, :, ds(h, 1)].rearrange("p t a -> p (t a)"), ALU.max)
                    eng.drain()
                    V.reciprocal(den, den)
                    eng.drain()
                    for t in range(TT):
                        V.tensor_scalar(mix[:, t, ds(h * M_DIM, M_DIM)], ps[:, 4 + t, 0:M_DIM], den[:, t:t + 1], None, ALU.mult)
                    eng.drain()

            if name in ("pe", "act", "dve"):
                with eng.Fori(0, M_HEADS) as h:
                    body(h)
            phase(name, eng)

        def rotate(dve, t1, t2, c, s, work, n):
            w = [work[i] for i in range(4)]
            V.tensor_tensor(w[0], t1, c, ALU.mult)
            V.tensor_tensor(w[1], t2, s, ALU.mult)
            V.tensor_tensor(w[2], t1, s, ALU.mult)
            V.tensor_tensor(w[3], t2, c, ALU.mult)
            dve.drain()
            V.tensor_tensor(t1, w[0], w[1], ALU.subtract)
            V.tensor_tensor(t2, w[2], w[3], ALU.add)
            dve.drain()

        k_lat = view(tmp, 4864, TT, A_HEADS * A_QK)
        cqT, ckvT = view(tmp, 0, 2, S), view(tmp, 2 * S, 1, S)
        lat_w = view(tmp, 0, TT, A_HEADS * A_QK)

        def latent_inputs(name, eng, l):
            cq, ckv = proj[:, :, OFF_CQ:OFF_CQ + A_Q_RANK], proj[:, :, OFF_CKV:OFF_CKV + A_KV_RANK]
            junk = view(tmp, 4864, A_Q_RANK)
            if name == "act":
                for t in range(TT):
                    A.activation(junk, cq[:, t, :], ACT.Square, accum_out=stat[:, t:t + 1])
                    eng.drain()
                    A.activation(junk[:, 0:A_KV_RANK], ckv[:, t, :], ACT.Square, accum_out=stat[:, 4 + t:5 + t])
                    eng.drain()
            phase(name, eng)
            if name == "pool":
                rsqrt(eng, stat[:, 0:4], A_Q_RANK)
                rsqrt(eng, stat[:, 4:8], A_KV_RANK)
            phase(name, eng)
            if name == "dve":
                for t in range(TT):
                    V.tensor_scalar(cq[:, t, :], cq[:, t, :], stat[:, t:t + 1], None, ALU.mult)
                    V.tensor_scalar(ckv[:, t, :], ckv[:, t, :], stat[:, 4 + t:5 + t], None, ALU.mult)
            phase(name, eng)
            if name == "pe":
                pe_banks(eng, turn_jobs(cq, 2) + turn_jobs(ckv, 1) + turn_jobs(ckv, 1))
            else:
                g = p1(l, "cq_g")
                reads = [copier(name, cqT[:, c, :], S, g[:, c:c + 1]) for c in range(2)]
                kv = copier(name, ckvT[:, 0, :], S, p1(l, "ckv_g"))
                spare = copier(name, view(tmp, 4096, S), S)
                read_banks(name, eng, reads + [kv, spare])
            phase(name, eng)
            w_uq = p1(l, "w_uq").rearrange("p (k n) -> p k n", k=2)
            w_ukv = p1(l, "w_ukv").rearrange("p (k n) -> p k n", k=1)
            outs = []
            for lhs, w, kc, dst, total in ((cqT, w_uq, 2, q_lat, A_HEADS * A_QK), (ckvT, w_ukv, 1, kv_lat, A_HEADS * A_KV)):
                half = total // 2
                for i in range(2):
                    for t in range(TT):
                        outs.append((lhs, w, kc, dst, half, i, t))
            if name == "pe":
                def job(lhs, w, kc, dst, half, i, t):
                    def run(bank):
                        for k in range(kc):
                            yield T.matmul(bank[:, 0:half], lhs[:, k, t * P:(t + 1) * P], w[:, k, i * half:(i + 1) * half],
                                           start=k == 0, stop=k == kc - 1)
                    return run
                pe_banks(eng, [job(*o) for o in outs])
            elif name in ("act", "dve"):
                read_banks(name, eng, [copier(name, dst[:, t, i * half:(i + 1) * half], half)
                                       for lhs, w, kc, dst, half, i, t in outs])
            phase(name, eng)
            ss = stat[:, 0:2 * TT * A_HEADS]
            if name == "dve":
                for t in range(TT):
                    kh = k_lat[:, t, :].rearrange("p (h w) -> p h w", w=A_QK)
                    V.tensor_copy(kh[:, :, 0:A_NOPE], kv_lat[:, t, :].rearrange("p (h w) -> p h w", w=A_KV)[:, :, 0:A_NOPE])
                    V.tensor_copy(kh[:, :, A_NOPE:], proj[:, t, OFF_KR:OFF_KR + A_ROPE].unsqueeze(1)
                                  .to_broadcast([P, A_HEADS, A_ROPE]))
                eng.drain()
                for i, src in enumerate((q_lat, k_lat)):
                    V.tensor_tensor(lat_w, src, src, ALU.mult)
                    eng.drain()
                    V.tensor_reduce(ss[:, i * 24:(i + 1) * 24], lat_w.rearrange("p t (h w) -> p (t h) w", w=A_QK), AX.X, ALU.add)
                    eng.drain()
            phase(name, eng)
            if name == "pool":
                rsqrt(eng, ss, A_QK)
            phase(name, eng)
            if name == "dve":
                for i, (src, gain) in enumerate(((q_lat, "qh_g"), (k_lat, "kh_g"))):
                    heads = src.rearrange("p t (h w) -> p (t h) w", w=A_QK)
                    V.tensor_tensor(heads, heads, ss[:, i * 24:(i + 1) * 24].unsqueeze(2).to_broadcast([P, 24, A_QK]), ALU.mult)
                    eng.drain()
                    V.tensor_tensor(heads, heads, p1(l, gain).unsqueeze(1).to_broadcast([P, 24, A_QK]), ALU.mult)
                    eng.drain()
                    for t in range(TT):
                        hh = src[:, t, :].rearrange("p (h w) -> p h w", w=A_QK)
                        half = A_ROPE // 2
                        c, s = (r[:, t, :].unsqueeze(1).to_broadcast([P, A_HEADS, half]) for r in (cos1, sin1))
                        work = [view(tmp, k * A_HEADS * half, A_HEADS, half) for k in range(4)]
                        rotate(eng, hh[:, :, A_NOPE:A_NOPE + half], hh[:, :, A_NOPE + half:], c, s, work, half)
            phase(name, eng)

        def latent_attention(name, eng, l):
            causal = c_("causal")
            attention(name, eng, dict(
                steps=A_HEADS, qd=A_QK, parts=A_QK, key_tiles=TT, vd=A_V, scale=float(A_QK) ** -0.5,
                q=lambda c: q_lat[:, :, ds(c * A_QK, A_QK)], k=lambda c: k_lat[:, :, ds(c * A_QK, A_QK)],
                v=lambda c, s, sub: kv_lat[:, s, ds(c * A_KV + A_NOPE, A_V)],
                mask=lambda t, width: causal[:, S - width:S],
                o=lambda c, t, sub: mix[:, t, ds(c * A_V + M_WIDTH, A_V)],
                units=[(0, A_QK, t, (t + 1) * P, 0) for t in range(TT)]))

        gate_u, gate_v = proj[:, :, OFF_CU:OFF_CU + C_WIDTH], proj[:, :, OFF_CV:OFF_CV + C_WIDTH]

        def spatial_gating(name, eng, l):
            sq = view(tmp, 0, TT, C_WIDTH)
            ss = stat[:, 0:TT * C_GROUPS]
            if name == "act":
                A.activation(gate_u, gate_u, ACT.Gelu_apprx_tanh)
                A.activation(gate_v, gate_v, ACT.Gelu_apprx_tanh)
                A.activation(proj[:, :, OFF_O:OFF_O + M_WIDTH], proj[:, :, OFF_O:OFF_O + M_WIDTH], ACT.Sigmoid)
            phase(name, eng)
            if name == "dve":
                V.tensor_tensor(mix[:, :, 0:M_WIDTH], mix[:, :, 0:M_WIDTH], proj[:, :, OFF_O:OFF_O + M_WIDTH], ALU.mult)
                V.tensor_tensor(sq, gate_v, gate_v, ALU.mult)
                eng.drain()
                V.tensor_reduce(ss, sq.rearrange("p t (g w) -> p (t g) w", w=C_DIM), AX.X, ALU.add)
                w_s = p1(l, "w_s").rearrange("p (g t) -> p g t", g=C_GROUPS)
                V.tensor_tensor(w_s, w_s, c_("upto").unsqueeze(1).to_broadcast([P, C_GROUPS, P]), ALU.mult)
            phase(name, eng)
            if name == "pool":
                rsqrt(eng, ss, C_DIM)
            phase(name, eng)
            if name == "dve":
                for t in range(TT):
                    vt = gate_v[:, t, :].rearrange("p (g w) -> p g w", w=C_DIM)
                    V.tensor_tensor(vt, vt, ss[:, t * C_GROUPS:(t + 1) * C_GROUPS].unsqueeze(2)
                                    .to_broadcast([P, C_GROUPS, C_DIM]), ALU.mult)
                eng.drain()
                V.tensor_tensor(gate_v, gate_v, p1(l, "cv_g").unsqueeze(1).to_broadcast([P, TT, C_WIDTH]), ALU.mult)
            phase(name, eng)
            if name == "pe":
                def job(g):
                    def run(bank):
                        for t in range(TT):
                            yield T.matmul(bank[:, t * C_DIM:(t + 1) * C_DIM], p1(l, "w_s")[:, g * P:(g + 1) * P],
                                           gate_v[:, t, g * C_DIM:(g + 1) * C_DIM], start=True, stop=True)
                    return run
                pe_banks(eng, [job(g) for g in range(C_GROUPS)])
            elif name in ("act", "dve"):
                mixed = view(tmp, 0, C_GROUPS, TT, C_DIM)
                reads = []
                for g in range(C_GROUPS):
                    bias = p1(l, "b_s")[:, g:g + 1]

                    def read(bank, g=g, bias=bias):
                        src = bank[:, 0:TT * C_DIM].rearrange("p (t w) -> p t w", w=C_DIM)
                        if name == "act":
                            return A.activation(mixed[:, g], src, ACT.Identity, bias=bias)
                        return V.tensor_scalar(mixed[:, g], src, bias, None, ALU.add)
                    reads.append(read)
                read_banks(name, eng, reads)
            phase(name, eng)
            if name == "dve":
                mixed = view(tmp, 0, C_GROUPS, TT, C_DIM)
                for g in range(C_GROUPS):
                    V.tensor_tensor(mix[:, :, M_WIDTH + A_HEADS * A_V + g * C_DIM:M_WIDTH + A_HEADS * A_V + (g + 1) * C_DIM],
                                    gate_u[:, :, g * C_DIM:(g + 1) * C_DIM], mixed[:, g], ALU.mult)
                eng.drain()

        def heads_out(name, eng, l):
            sq = view(tmp, 0, TT, D)
            parts = ((0, M_HEADS, M_DIM), (M_WIDTH, A_HEADS, A_V), (M_WIDTH + A_HEADS * A_V, C_GROUPS, C_DIM))
            if name == "dve":
                V.tensor_tensor(sq, mix, mix, ALU.mult)
                eng.drain()
                for i, (o, h, w) in enumerate(parts):
                    for t in range(TT):
                        V.tensor_reduce(stat[:, i * 24 + t * h:i * 24 + (t + 1) * h],
                                        sq[:, t, o:o + h * w].rearrange("p (h w) -> p h w", w=w), AX.X, ALU.add)
            phase(name, eng)
            if name == "pool":
                for i, (o, h, w) in enumerate(parts):
                    rsqrt(eng, stat[:, i * 24:i * 24 + TT * h], w)
            phase(name, eng)
            if name == "dve":
                for i, (o, h, w) in enumerate(parts):
                    for t in range(TT):
                        v = mix[:, t, o:o + h * w].rearrange("p (h w) -> p h w", w=w)
                        V.tensor_tensor(v, v, stat[:, i * 24 + t * h:i * 24 + (t + 1) * h].unsqueeze(2)
                                        .to_broadcast([P, h, w]), ALU.mult)
            phase(name, eng)
            turn(name, eng, mix, featv, KC, p1(l, "out_g"))
            y = view(tmp, 0, TT, D)
            project(name, eng, featv, [512, 512], y)
            if name == "dve":
                V.tensor_tensor(x, x, y, ALU.add)
            phase(name, eng)

        logits = view(tmp, 4096, TT, N_GROUPS + N_EXP)
        LW = 4096 + TT * (N_GROUPS + N_EXP)
        hot1, hot2 = view(tmp, LW, TT, N_EXP), view(tmp, LW + 128, TT, N_EXP)
        member, slot_of = view(tmp, LW + 256, TT, N_EXP), view(tmp, LW + 384, TT, N_EXP)
        r_work = LW + 512
        weight = stat[:, 128:136]
        dest_i, dest_t = route_i[:, 0:8], route_i[:, 8:16]
        slots_tok = route_i[:, 16:16 + TABLE_W]
        blk_exp = route_i[:, 16 + TABLE_W:16 + TABLE_W + N_BLK]
        tok_id = route_i[:, 16 + TABLE_W + N_BLK:R_IDX]

        def first_max(dve, src, n, hot, at):
            top, cand = view(tmp, at, TT), view(tmp, at + 8, TT, n)
            V.tensor_reduce(top, src, AX.X, ALU.max)
            dve.drain()
            V.tensor_tensor(cand, src, top.unsqueeze(2).to_broadcast([P, TT, n]), ALU.is_equal)
            dve.drain()
            V.scalar_tensor_tensor(out=cand, in0=cand, scalar=-64.0,
                                   in1=c_("iota")[:, 0:n].unsqueeze(1).to_broadcast([P, TT, n]), op0=ALU.mult, op1=ALU.add)
            dve.drain()
            V.tensor_reduce(top, cand, AX.X, ALU.min)
            dve.drain()
            V.tensor_tensor(hot, cand, top.unsqueeze(2).to_broadcast([P, TT, n]), ALU.is_equal)
            dve.drain()

        def router(name, eng, l):
            w = p1(l, "w_route").rearrange("p (k n) -> p k n", k=KC)
            n = N_GROUPS + N_EXP
            if name == "pe":
                def job(t):
                    def run(bank):
                        for k in range(KC):
                            yield T.matmul(bank[:, 0:n], featv[:, k, t * P:(t + 1) * P], w[:, k, :], start=k == 0, stop=k == KC - 1)
                    return run
                pe_banks(eng, [job(t) for t in range(TT)])
            elif name in ("act", "dve"):
                read_banks(name, eng, [copier(name, logits[:, t, :], n) for t in range(TT)])
            phase(name, eng)
            W = r_work + 256
            g_hot, g_e, e_sel, e_b = view(tmp, W, TT, 4), view(tmp, W + 16, TT, 4), view(tmp, W + 32, TT, 8), view(tmp, W + 64, TT, 8)
            h1, h2, work8 = view(tmp, W + 96, TT, 8), view(tmp, W + 128, TT, 8), view(tmp, W + 160, TT, 8)
            c1, c2 = view(tmp, W + 192, TT), view(tmp, W + 196, TT)
            gate, s1, s2 = view(tmp, W + 200, TT), view(tmp, W + 204, TT), view(tmp, W + 208, TT)
            if name == "dve":
                g_raw = logits[:, :, 0:N_GROUPS]
                V.tensor_tensor(g_e, g_raw, p1(l, "group_b").unsqueeze(1).to_broadcast([P, TT, 4]), ALU.add)
                eng.drain()
                first_max(eng, g_e, N_GROUPS, g_hot, r_work)
                V.tensor_reduce(c1, g_raw, AX.X, ALU.max)
                eng.drain()
                V.tensor_tensor(g_e, g_raw, c1.unsqueeze(2).to_broadcast([P, TT, 4]), ALU.subtract)
                for g in range(N_GROUPS):
                    pick = g_hot[:, :, g:g + 1].to_broadcast([P, TT, 8])
                    raw = logits[:, :, N_GROUPS + g * 8:N_GROUPS + (g + 1) * 8]
                    bias = p1(l, "exp_b")[:, g * 8:(g + 1) * 8].unsqueeze(1).to_broadcast([P, TT, 8])
                    if g == 0:
                        V.tensor_tensor(e_sel, raw, pick, ALU.mult)
                        V.tensor_tensor(e_b, bias, pick, ALU.mult)
                        eng.drain()
                        continue
                    V.tensor_tensor(work8, raw, pick, ALU.mult)
                    eng.drain()
                    V.tensor_tensor(e_sel, e_sel, work8, ALU.add)
                    eng.drain()
                    V.tensor_tensor(work8, bias, pick, ALU.mult)
                    eng.drain()
                    V.tensor_tensor(e_b, e_b, work8, ALU.add)
                    eng.drain()
                V.tensor_tensor(e_b, e_b, e_sel, ALU.add)
                eng.drain()
                first_max(eng, e_b, PER_GROUP, h1, r_work)
                V.scalar_tensor_tensor(out=e_b, in0=h1, scalar=-1e30, in1=e_b, op0=ALU.mult, op1=ALU.add)
                eng.drain()
                first_max(eng, e_b, PER_GROUP, h2, r_work)
                V.tensor_reduce(c1, e_sel, AX.X, ALU.max)
                eng.drain()
                V.tensor_tensor(e_sel, e_sel, c1.unsqueeze(2).to_broadcast([P, TT, 8]), ALU.subtract)
            phase(name, eng)
            if name == "act":
                A.activation(g_e, g_e, ACT.Exp)
                A.activation(e_sel, e_sel, ACT.Exp)
            phase(name, eng)
            if name == "dve":
                V.tensor_reduce(s1, g_e, AX.X, ALU.add)
                eng.drain()
                V.tensor_tensor(g_e, g_e, g_hot, ALU.mult)
                eng.drain()
                V.tensor_reduce(gate, g_e, AX.X, ALU.add)
                V.reciprocal(s1, s1)
                eng.drain()
                V.tensor_tensor(gate, gate, s1, ALU.mult)
                for hh, out in ((h1, c1), (h2, c2)):
                    V.tensor_tensor(work8, e_sel, hh, ALU.mult)
                    eng.drain()
                    V.tensor_reduce(out, work8, AX.X, ALU.add)
                    eng.drain()
                V.tensor_tensor(s2, c1, c2, ALU.add)
                eng.drain()
                V.reciprocal(s2, s2)
                eng.drain()
                V.tensor_tensor(gate, gate, s2, ALU.mult)
                eng.drain()
                V.tensor_tensor(weight[:, 0:TT], gate, c1, ALU.mult)
                V.tensor_tensor(weight[:, TT:2 * TT], gate, c2, ALU.mult)
                for hh, hot in ((h1, hot1), (h2, hot2)):
                    for g in range(N_GROUPS):
                        V.tensor_tensor(hot[:, :, g * 8:(g + 1) * 8], hh, g_hot[:, :, g:g + 1].to_broadcast([P, TT, 8]), ALU.mult)
                eng.drain()
                V.tensor_tensor(member, hot1, hot2, ALU.add)
            phase(name, eng)
            if name == "pe":
                def ejob(t):
                    def run(bank):
                        for s in range(t):
                            yield T.matmul(bank[:, 0:N_EXP], c_("ones"), member[:, s, :], start=s == 0, stop=False)
                        yield T.matmul(bank[:, 0:N_EXP], c_("before"), member[:, t, :], start=t == 0, stop=True)
                    return run

                def ajob(bank):
                    for s in range(TT):
                        yield T.matmul(bank[:, 0:N_EXP], c_("ones"), member[:, s, :], start=s == 0, stop=s == TT - 1)
                pe_banks(eng, [ejob(t) for t in range(TT)] + [ajob, ajob])
            cnt, blocks, ends, start = (view(tmp, r_work + 32 * i, N_EXP) for i in range(4))
            if name in ("act", "dve"):
                read_banks(name, eng, [copier(name, slot_of[:, t, :], N_EXP) for t in range(TT)]
                           + [copier(name, cnt, N_EXP), copier(name, start, N_EXP)])
            phase(name, eng)
            if name == "dve":
                ones32 = c_("ones")[:, 0:N_EXP]
                V.tensor_scalar(blocks, cnt, 0.0, None, ALU.is_gt)
                eng.drain()
                for k in range(1, TT):
                    V.tensor_scalar(ends, cnt, float(P * k), None, ALU.is_gt)
                    eng.drain()
                    V.tensor_tensor(blocks, blocks, ends, ALU.add)
                    eng.drain()
                V.tensor_tensor_scan(ends, ones32, blocks, 0.0, ALU.mult, ALU.add)
                eng.drain()
                V.tensor_tensor(start, ends, blocks, ALU.subtract)
                eng.drain()
                V.tensor_scalar(start, start, float(P), None, ALU.mult)
                eng.drain()
                V.tensor_tensor(slot_of, slot_of, start.unsqueeze(1).to_broadcast([P, TT, N_EXP]), ALU.add)
                eng.drain()
                dest = stat[:, 136:144]
                for i, hot in enumerate((hot1, hot2)):
                    V.tensor_tensor(hot, hot, slot_of, ALU.mult)
                    eng.drain()
                    V.tensor_reduce(dest[:, i * TT:(i + 1) * TT], hot, AX.X, ALU.add)
                eng.drain()
                V.tensor_copy(dest_i, dest)
                eng.drain()
                low, high = view(stat, 144, 8).bitcast(i32), view(stat, 152, 8).bitcast(i32)
                V.tensor_scalar(low, dest_i, P - 1, None, ALU.bitwise_and)
                V.tensor_scalar(high, dest_i, 7, None, ALU.logical_shift_right)
                eng.drain()
                V.tensor_scalar(stat[:, 160:168], low, float(TABLE_W), None, ALU.mult)
                V.tensor_copy(stat[:, 168:176], high)
                eng.drain()
                V.tensor_tensor(dest_t, stat[:, 160:168], stat[:, 168:176], ALU.add)
                table = view(tmp, 8 * D, N_BLK, N_EXP)
                V.tensor_tensor(table, ends.unsqueeze(1).to_broadcast([P, N_BLK, N_EXP]),
                                c_("blocks").unsqueeze(2).to_broadcast([P, N_BLK, N_EXP]), ALU.is_le)
                V.tensor_scalar(turns_used, ends[:, N_EXP - 1:N_EXP], 1.0, None, ALU.add)
                eng.drain()
                bf = view(tmp, r_work, N_BLK)
                V.tensor_reduce(bf, table, AX.X, ALU.add)
                eng.drain()
                V.tensor_scalar(blk_exp, bf, float(N_EXP - 1), None, ALU.min)
            phase(name, eng)

        table_d, table_rows = a["slot_table"], a["slot_table"].rearrange("(n a) -> n a", a=1)
        xn = view(tmp, 0, TT, D)

        def share_rows(name, eng, l):
            if name == "pool":
                G.memset(slots_tok, 0)
                eng.drain()
                eng.dma_start(a["normed"].rearrange("(t p) d -> p t d", p=P), xn).then_inc(normed_out, 16)
                eng.dma_start(table_d.rearrange("(p n) -> p n", p=P), slots_tok).then_inc(table_zeroed, 16)

        def fill_table(name, eng, l):
            if name == "pool":
                eng.wait_ge(table_zeroed, 16 * (l + 1))
                eng.wait_ge(normed_out, 16 * (l + 1))
                for i in range(2):
                    for t in range(TT):
                        j = i * TT + t
                        eng.indirect_dma_start(out=table_rows, out_offset=bass.IndirectOffsetOnAxis(ap=dest_t[:, j:j + 1], axis=0),
                                               in_=tok_id[:, t:t + 1], in_offset=None).then_inc(table_filled, 16)
                eng.wait_ge(table_filled, 16 * 2 * TT * (l + 1))
                eng.dma_start(slots_tok, table_d.rearrange("(p n) -> p n", p=P)).then_inc(table_read, 16)
                eng.wait_ge(table_read, 16 * (l + 1))
            phase(name, eng)

        e_w = [ring[:, 0:6144], big[:, 0:6144], big[:, 6144:12288]]
        e_x = [view(tmp, s * D, D) for s in range(E_SLOTS)]
        e_y = [view(tmp, (3 + s) * D, D) for s in range(E_SLOTS)]
        e_xT = [view(tmp, (6 + s) * D, KC, P) for s in range(E_SLOTS)]
        e_sg, e_h, e_hT = view(tmp, 9 * D, D_EXP), view(tmp, 9 * D + 256, D_EXP), view(tmp, 9 * D + 512, 2, P)
        turns_used = route_i[:, R_IDX + E_SLOTS:R_IDX + E_SLOTS + 1]
        e_idx = [route_i[:, R_IDX + s:R_IDX + s + 1] for s in range(E_SLOTS)]

        def up_w(s):
            return e_w[s][:, 0:KC * 2 * D_EXP].rearrange("p (k n) -> p k n", k=KC)

        def down_w(s):
            return e_w[s][:, KC * 2 * D_EXP:].rearrange("p (k n) -> p k n", k=2)

        def experts(name, eng, l):
            base = l * E_STEPS + 1

            def before(s, n):
                return (s - 1) % E_SLOTS, n if s else n - 1

            def rows_count(s, n):
                return n if s else n + l

            def turn_rows(s, n):
                m = rows_count(s, n)
                eng.wait_ge(e_rows[s], 16 * m)
                for k in range(KC):
                    last = T.transpose(ps[:, k // 4, (k % 4) * P:(k % 4 + 1) * P], e_x[s][:, k * P:(k + 1) * P], ident)
                last.then_inc(e_turned[s], 1)

            def copy_rows(s, n):
                m = rows_count(s, n)
                eng.wait_ge(e_turned[s], m + 1)
                g = p1(l, "ffn_g")
                for b in range(2):
                    last = V.tensor_tensor(e_xT[s][:, 4 * b:4 * b + 4, :], ps[:, b, :].rearrange("p (k s) -> p k s", k=4),
                                           g[:, 4 * b:4 * b + 4].unsqueeze(2).to_broadcast([P, 4, P]), ALU.mult)
                last.then_inc(e_rowsT[s], 1)

            def gather_rows(s, n, blk):
                m = rows_count(s, n)
                eng.wait_ge(e_turned[s], m)
                G.tensor_copy(e_idx[s], slots_tok[:, ds(blk, 1)])
                eng.drain()
                eng.indirect_dma_start(out=e_x[s], out_offset=None, in_=a["normed"],
                                       in_offset=bass.IndirectOffsetOnAxis(ap=e_idx[s], axis=0)).then_inc(e_rows[s], 16)

            def down(s, n):
                s2, n2 = before(s, n)
                eng.wait_ge(e_hiddenT[s], n + 1)
                eng.wait_ge(e_copied[s2], n2 + 1)
                for half in range(2):
                    for k in range(2):
                        last = T.matmul(ps[:, 4 + half, :], e_hT[:, k, :], down_w(s)[:, k, half * BANK:(half + 1) * BANK],
                                        start=k == 0, stop=k == 1)
                last.then_inc(e_down[s], 1)

            def store(s, n, blk):
                eng.wait_ge(e_down[s], n + 1)
                eng.wait_ge(e_stored[s], 16 * n)
                A.activation(e_y[s], ps[:, 4:6, :].rearrange("p b n -> p (b n)"), ACT.Copy).then_inc(e_copied[s], 1)
                eng.wait_ge(e_copied[s], n + 1)
                eng.dma_start(a["expert_out"][ds(blk * P, P), :], e_y[s]).then_inc(e_stored[s], 16)

            def body(i, first=False):
                n = i + base
                for s in range(E_SLOTS):
                    blk = i * E_SLOTS + s
                    nxt = (s + 1) % E_SLOTS
                    n_nxt = n if nxt else n + 1
                    if name == "pool":
                        gather_rows(nxt, n_nxt, blk + 1)
                    elif first:
                        turn_work(s, n, blk, nxt, n_nxt, first)
                    else:
                        with eng.If(blk < used):
                            turn_work(s, n, blk, nxt, n_nxt, first)
                        with eng.Else():
                            turn_passed(s, n, blk, nxt, n_nxt)

            def turn_passed(s, n, blk, nxt, n_nxt):
                s2, n2 = before(s, n)
                if name == "sp":
                    eng.wait_ge(e_down[s], n)
                    eng.dma_start(e_w[s][0:16, 0:8], a["w13"][l, 0, 0:16, 0:8]).then_inc(e_loaded[s], 16)
                    eng.dma_start(e_w[s][16:32, 0:8], a["w13"][l, 0, 16:32, 0:8]).then_inc(e_loaded[s], 16)
                if name == "pe":
                    eng.wait_ge(e_loaded[s], 32 * n)
                    eng.wait_ge(e_rows[nxt], 16 * rows_count(nxt, n_nxt))
                    for p in (e_up[s], e_down[s2], e_hturned[s], e_turned[nxt]):
                        eng.sem_inc(p, 1)
                if name == "dve":
                    eng.wait_ge(e_turned[nxt], rows_count(nxt, n_nxt) + 1)
                    for p in (e_hidden[s], e_hiddenT[s], e_rowsT[nxt]):
                        eng.sem_inc(p, 1)
                if name == "act":
                    eng.wait_ge(e_down[s2], n2 + 1)
                    eng.wait_ge(e_stored[s2], 16 * n2)
                    eng.sem_inc(e_silu[s], 1)
                    eng.sem_inc(e_copied[s2], 1)
                    eng.dma_start(a["expert_out"][ds((blk - 1) * P, P), :], e_y[s2]).then_inc(e_stored[s2], 16)

            def turn_work(s, n, blk, nxt, n_nxt, first):
                if name == "sp":
                    eng.wait_ge(e_down[s], n)
                    e = eng.value_load(blk_exp[0:1, ds(blk, 1)], min_val=0, max_val=N_EXP - 1)
                    eng.dma_start(e_w[s][:, 0:KC * 2 * D_EXP], a["w13"][l, ds(e, 1), :, :].rearrange("a p n -> p (a n)")).then_inc(e_loaded[s], 16)
                    eng.dma_start(e_w[s][:, KC * 2 * D_EXP:], a["w2"][l, ds(e, 1), :, :].rearrange("a p n -> p (a n)")).then_inc(e_loaded[s], 16)
                if name == "pe":
                    eng.wait_ge(e_loaded[s], 32 * n)
                    eng.wait_ge(e_rowsT[s], rows_count(s, n) + 1)
                    for k in range(KC):
                        m = T.matmul(ps[:, 2, :], e_xT[s][:, k, :], up_w(s)[:, k, :], start=k == 0, stop=k == KC - 1)
                    m.then_inc(e_up[s], 1)
                    if not (first and s == 0):
                        down(*before(s, n))
                    eng.wait_ge(e_hidden[s], n + 1)
                    for k in range(2):
                        m = T.transpose(ps[:, 3, k * P:(k + 1) * P], e_h[:, k * P:(k + 1) * P], ident)
                    m.then_inc(e_hturned[s], 1)
                    turn_rows(nxt, n_nxt)
                if name == "dve":
                    eng.wait_ge(e_silu[s], n + 1)
                    V.tensor_tensor(e_h, e_sg, ps[:, 2, D_EXP:2 * D_EXP], ALU.mult).then_inc(e_hidden[s], 1)
                    eng.wait_ge(e_hturned[s], n + 1)
                    V.tensor_copy(e_hT, ps[:, 3, 0:2 * P].rearrange("p (k s) -> p k s", k=2)).then_inc(e_hiddenT[s], 1)
                    copy_rows(nxt, n_nxt)
                if name == "act":
                    eng.wait_ge(e_up[s], n + 1)
                    A.activation(e_sg, ps[:, 2, 0:D_EXP], ACT.Silu).then_inc(e_silu[s], 1)
                    if not (first and s == 0):
                        store(*before(s, n), blk - 1)

            if name == "pool":
                gather_rows(0, base, 0)
            if name == "pe":
                turn_rows(0, base)
            if name == "dve":
                copy_rows(0, base)
            body(0, first=True)
            used = None if name == "pool" else eng.value_load(turns_used[0:1, 0:1], min_val=2, max_val=N_BLK + 1)
            with eng.Fori(1, E_STEPS) as i:
                body(i)
            if name == "pe":
                down(E_SLOTS - 1, base + E_STEPS - 1)
            if name == "act":
                store(E_SLOTS - 1, base + E_STEPS - 1, N_BLK - 1)
                for s in range(E_SLOTS):
                    eng.wait_ge(e_stored[s], 16 * (base + E_STEPS))

        def combine(name, eng, l):
            got = [view(tmp, k * D, D) for k in range(2 * TT)]
            if name == "pool":
                for j in range(2 * TT):
                    eng.indirect_dma_start(out=got[j], out_offset=None, in_=a["expert_out"],
                                           in_offset=bass.IndirectOffsetOnAxis(ap=dest_i[:, j:j + 1], axis=0)
                                           ).then_inc(pair_loaded[0], 16)
                eng.wait_ge(pair_loaded[0], 16 * 2 * TT * (l + 1))
            phase(name, eng)
            if name == "dve":
                for i in range(2):
                    for t in range(TT):
                        j = i * TT + t
                        V.scalar_tensor_tensor(out=x[:, t, :], in0=got[j], scalar=weight[:, j:j + 1], in1=x[:, t, :],
                                               op0=ALU.mult, op1=ALU.add)
                    eng.drain()
            phase(name, eng)

        qkv = view(big, 0, TT, 3 * D)

        def rotate_partial(name, eng, l):
            half = ROT // 2
            if name == "dve":
                for t in range(TT):
                    hh = qkv[:, t, 0:2 * D].rearrange("p (h w) -> p h w", w=HD)
                    n = 2 * D // HD
                    c, s = (r[:, t, :].unsqueeze(1).to_broadcast([P, n, half]) for r in (cos2, sin2))
                    work = [view(tmp, k * n * half, n, half) for k in range(4)]
                    rotate(eng, hh[:, :, 0:half], hh[:, :, half:ROT], c, s, work, half)
            phase(name, eng)

        def dilated(name, eng, l):
            m = c_("dilated").rearrange("p (t s) -> p t s", t=TT)
            attention(name, eng, dict(
                steps=KC, qd=P, parts=P, key_tiles=TT, vd=HD, scale=float(HD) ** -0.5,
                q=lambda c: qkv[:, :, ds(c * P, P)], k=lambda c: qkv[:, :, ds(c * P + D, P)],
                v=lambda c, s, sub: qkv[:, s, ds(c * P + 2 * D + sub * HD, HD)],
                mask=lambda t, width: m[:, t, :],
                o=lambda c, t, sub: qkv[:, t, ds(c * P + sub * HD, HD)],
                units=[(sub * HD, (sub + 1) * HD, t, S, sub) for sub in range(2) for t in range(TT)]))

        neg_lam = stat[:, 200:201]
        sub_ss = view(stat, 204, TT * KC)

        def differential(name, eng, l):
            lam = p2(1, "lam").rearrange("p (a w) -> p a w", a=4)
            pair = stat[:, 201:203]
            if name == "dve":
                V.tensor_tensor(lam[:, 0, :], lam[:, 0, :], lam[:, 1, :], ALU.mult)
                V.tensor_tensor(lam[:, 2, :], lam[:, 2, :], lam[:, 3, :], ALU.mult)
                eng.drain()
                V.tensor_reduce(stat[:, 201:202], lam[:, 0, :], AX.X, ALU.add)
                V.tensor_reduce(stat[:, 202:203], lam[:, 2, :], AX.X, ALU.add)
            phase(name, eng)
            if name == "act":
                A.activation(pair, pair, ACT.Exp)
            phase(name, eng)
            if name == "dve":
                V.tensor_tensor(neg_lam, stat[:, 202:203], stat[:, 201:202], ALU.subtract)
                eng.drain()
                V.tensor_scalar(neg_lam, neg_lam, -LAM_INIT, None, ALU.add)
            phase(name, eng)
            c0, b0 = take(name, "diff_step", KC), take(name, "diff_unit", KC * TT)
            qs, ks = view(tmp, 0, TT, P), view(tmp, 512, TT, P)
            qT, kT = view(tmp, 1024, S), view(tmp, 1536, S)
            prob = [view(tmp, 2048 + i * 1024, 2, S) for i in range(2)]
            diff = [view(tmp, 4096 + i * 512, S) for i in range(2)]
            probT = [view(tmp, 5120 + i * 512, TT, P) for i in range(2)]
            nmax = view(stat, 16, 2, 2)
            rsum = view(stat, 20, 2, 2)
            scale = float(HD) ** -0.5

            def stage_heads(c):
                if name == "dve":
                    V.tensor_copy(qs, qkv[:, :, ds(c * P, P)])
                    V.tensor_copy(ks, qkv[:, :, ds(c * P + D, P)]).then_inc(d_staged, 1)

            def turn_heads(c):
                n = c0 + c + 1
                if name == "dve":
                    eng.wait_ge(d_turned, n)
                    V.tensor_copy(kT, ps[:, 7, :]).then_inc(d_kT, 1)
                if name == "pe":
                    eng.wait_ge(d_staged, n)
                    for bank, src in ((6, qs), (7, ks)):
                        for t in range(TT):
                            m = T.transpose(ps[:, bank, t * P:(t + 1) * P], src[:, t, :], ident)
                    m.then_inc(d_turned, 1)
                if name == "act":
                    eng.wait_ge(d_turned, n)
                    A.activation(qT, ps[:, 6, :], ACT.Copy).then_inc(d_qT, 1)

            def body(c, more=True):
                n, b = c0 + c + 1, b0 + c * TT
                if name == "pe":
                    eng.wait_ge(d_qT, n)
                    eng.wait_ge(d_kT, n)

                def scores(t):
                    if t >= 2:
                        eng.wait_ge(d_probs, b + t - 1)
                    for j in range(2):
                        m = T.matmul(ps[:, (t % 2) * 2 + j, :], qT[j * HD:(j + 1) * HD, t * P:(t + 1) * P],
                                     kT[j * HD:(j + 1) * HD, :], start=True, stop=True)
                    m.then_inc(d_scores, 1)

                def maximum(t):
                    eng.wait_ge(d_scores, b + t + 1)
                    if t >= 2:
                        eng.wait_ge(d_probs, b + t - 1)
                    for j in range(2):
                        V.tensor_reduce(nmax[:, t % 2, j:j + 1], ps[:, (t % 2) * 2 + j, :], AX.X, ALU.max, negate=True)
                    eng.drain()
                    V.tensor_scalar(nmax[:, t % 2, :], nmax[:, t % 2, :], scale, None, ALU.mult).then_inc(d_max, 1)

                def expo(t):
                    eng.wait_ge(d_max, b + t + 1)
                    if t >= 2:
                        eng.wait_ge(d_mixed, b + t - 1)
                    for j in range(2):
                        m = A.activation(prob[t % 2][:, j, :], ps[:, (t % 2) * 2 + j, :], ACT.Exp, bias=nmax[:, t % 2, j:j + 1],
                                         scale=scale, accum_out=rsum[:, t % 2, j:j + 1])
                    m.then_inc(d_probs, 1)

                def mixed(t):
                    eng.wait_ge(d_probs, b + t + 1)
                    if t >= 2:
                        eng.wait_ge(d_full, b + t - 1)
                    r = rsum[:, t % 2, :]
                    V.reciprocal(r, r)
                    eng.drain()
                    V.tensor_scalar(r[:, 1:2], r[:, 1:2], neg_lam, None, ALU.mult)
                    V.tensor_scalar(diff[t % 2], prob[t % 2][:, 0, :], r[:, 0:1], None, ALU.mult)
                    eng.drain()
                    V.scalar_tensor_tensor(out=diff[t % 2], in0=prob[t % 2][:, 1, :], scalar=r[:, 1:2], in1=diff[t % 2],
                                           op0=ALU.mult, op1=ALU.add).then_inc(d_mixed, 1)

                def turn_diff(t):
                    eng.wait_ge(d_mixed, b + t + 1)
                    if t >= 1:
                        eng.wait_ge(d_probT, b + t)
                    for s in range(TT):
                        m = T.transpose(ps[:, 4, s * P:(s + 1) * P], diff[t % 2][:, s * P:(s + 1) * P], ident)
                    m.then_inc(d_full, 1)

                def copyT(t):
                    eng.wait_ge(d_full, b + t + 1)
                    if t >= 2:
                        eng.wait_ge(d_out, b + t - 1)
                    A.activation(probT[t % 2], ps[:, 4, :].rearrange("p (a s) -> p a s", s=P), ACT.Copy).then_inc(d_probT, 1)

                def output(t):
                    eng.wait_ge(d_probT, b + t + 1)
                    if t >= 1:
                        eng.wait_ge(d_read, b + t)
                    for s in range(TT):
                        m = T.matmul(ps[:, 5, 0:P], probT[t % 2][:, s, :], qkv[:, s, ds(c * P + 2 * D, P)],
                                     start=s == 0, stop=s == TT - 1)
                    m.then_inc(d_out, 1)

                def final(t):
                    eng.wait_ge(d_out, b + t + 1)
                    V.tensor_scalar(qkv[:, t, ds(c * P, P)], ps[:, 5, 0:P], 1.0, None, ALU.mult).then_inc(d_read, 1)

                stages = {"pe": ((0, scores), (2, turn_diff), (3, output)), "dve": ((0, maximum), (1, mixed), (3, final)),
                          "act": ((0, expo), (2, copyT))}[name]
                for u in range(TT + 3):
                    for lag, stage in stages:
                        if 0 <= u - lag < TT:
                            stage(u - lag)
                        if name == "pe" and lag == 0 and u == TT - 1 and more:
                            turn_heads(c + 1)
                    if u == 1 and more:
                        stage_heads(c + 1)
                    if u == TT - 1 and more and name != "pe":
                        turn_heads(c + 1)

            if name in ("pe", "act", "dve"):
                stage_heads(0)
                turn_heads(0)
                with eng.Fori(0, KC - 1) as c:
                    body(c)
                body(KC - 1, more=False)
            phase(name, eng)
            o = qkv[:, :, 0:D]
            sq = view(tmp, 0, TT, D)
            small, scaled = stat[:, 64:96], stat[:, 96:128]
            if name == "dve":
                V.tensor_scalar(sq, o, 1e15, -1e15, ALU.min, ALU.max)
                eng.drain()
                V.tensor_tensor(sq, sq, sq, ALU.mult)
                eng.drain()
                V.tensor_reduce(small, sq.rearrange("p t (h w) -> p (t h) w", w=P), AX.X, ALU.add)
                eng.drain()
                V.tensor_scalar(sq, o, 2.0 ** -66, None, ALU.mult)
                eng.drain()
                V.tensor_tensor(sq, sq, sq, ALU.mult)
                eng.drain()
                V.tensor_reduce(scaled, sq.rearrange("p t (h w) -> p (t h) w", w=P), AX.X, ALU.add)
                eng.drain()
                V.tensor_scalar(stat[:, 136:168], scaled, 2.0 ** -60, None, ALU.is_ge)
                V.tensor_scalar(stat[:, 168:200], scaled, 2.0 ** -4, None, ALU.is_lt)
                eng.drain()
                V.tensor_scalar(scaled, scaled, 2.0 ** -60, None, ALU.max)
            phase(name, eng)
            if name == "pool":
                half = stat[:, 255:256]
                G.tensor_scalar(small, small, 1.0 / P, EPS, ALU.mult, ALU.add)
                G.tensor_scalar(scaled, scaled, 1.0 / P, None, ALU.mult)
                eng.drain()
                G.tensor_tensor(out=small, in0=small, in1=bcast(half, [P, 32]), op=ALU.pow)
                G.tensor_tensor(out=scaled, in0=scaled, in1=bcast(half, [P, 32]), op=ALU.pow)
            phase(name, eng)
            if name == "dve":
                use, fits = stat[:, 136:168], stat[:, 168:200]
                V.tensor_scalar(scaled, scaled, 2.0 ** -66, None, ALU.mult)
                eng.drain()
                V.tensor_tensor(scaled, scaled, fits, ALU.mult)
                eng.drain()
                V.tensor_tensor(scaled, scaled, small, ALU.subtract)
                eng.drain()
                V.tensor_tensor(scaled, scaled, use, ALU.mult)
                eng.drain()
                V.tensor_tensor(small, small, scaled, ALU.add)
                eng.drain()
                V.tensor_scalar(small, small, 1.0 - LAM_INIT, None, ALU.mult)
                eng.drain()
                for t in range(TT):
                    v = o[:, t, :].rearrange("p (h w) -> p h w", w=P)
                    V.tensor_tensor(v, v, small[:, t * KC:(t + 1) * KC].unsqueeze(2).to_broadcast([P, KC, P]), ALU.mult)
            phase(name, eng)

        def add_normed(name, eng, y, gain):
            sq, scaled = view(tmp, 4096, D), view(tmp, 5120, TT, D)
            ss = stat[:, 0:TT]
            if name == "act":
                for t in range(TT):
                    A.activation(sq, y[:, t, :], ACT.Square, accum_out=ss[:, t:t + 1])
                    eng.drain()
            if name == "dve":
                V.tensor_tensor(scaled, y, gain.unsqueeze(1).to_broadcast([P, TT, D]), ALU.mult)
            phase(name, eng)
            if name == "pool":
                rsqrt(eng, ss, D)
            phase(name, eng)
            if name == "dve":
                for t in range(TT):
                    V.scalar_tensor_tensor(out=x[:, t, :], in0=scaled[:, t, :], scalar=ss[:, t:t + 1], in1=x[:, t, :],
                                           op0=ALU.mult, op1=ALU.add)
            phase(name, eng)

        y_out = view(tmp, 0, TT, D)

        def mixer(name, eng, l):
            project(name, eng, featv, [512] * 6, qkv)
            rotate_partial(name, eng, l)
            if l == 0:
                dilated(name, eng, l)
                turn(name, eng, qkv, featv, KC)
            else:
                differential(name, eng, l)
                turn(name, eng, qkv, featv, KC, bcast(p2(l, "sub_g"), [P, KC]))
            project(name, eng, featv, [512] * 2, y_out)
            add_normed(name, eng, y_out, p2(l, "mix_post"))

        mem = view(big, 8192, MT, D)
        kv_mem = view(big, 0, MT, 2 * D)
        q_mem = view(big, 4096, TT, D)
        memT = view(tmp, 4096, KC, N_MEM)

        def memory_attention(name, eng, l):
            if name == "pool":
                eng.dma_start(mem, a["mem"].rearrange("(t p) d -> p t d", p=P)).then_inc(mem_loaded, 16)
                eng.wait_ge(mem_loaded, 16 * (l + 1))
            phase(name, eng)
            norm(name, eng, mem, view(tmp, 0, MT, D), memT, p2(l, "memkv_g"), tiles=MT)
            project(name, eng, memT, [512] * 4, kv_mem, tiles=MT)
            norm(name, eng, x, view(tmp, 0, TT, D), featv, p2(l, "mem_g"))
            project(name, eng, featv, [512] * 2, q_mem)
            attention(name, eng, dict(
                steps=X_HEADS, qd=X_DIM, parts=P, key_tiles=MT, vd=X_DIM, scale=float(X_DIM) ** -0.5, mask=None,
                q=lambda c: q_mem[:, :, ds(c * X_DIM, X_DIM)], k=lambda c: kv_mem[:, :, ds(c * X_DIM, X_DIM)],
                v=lambda c, s, sub: kv_mem[:, s, ds(c * X_DIM + D, X_DIM)],
                o=lambda c, t, sub: q_mem[:, t, ds(c * X_DIM, X_DIM)],
                units=[(0, P, t, N_MEM, 0) for t in range(TT)]))
            turn(name, eng, q_mem, featv, KC)
            project(name, eng, featv, [512] * 2, y_out)
            add_normed(name, eng, y_out, p2(l, "mem_post"))

        hidden = view(tmp, 0, FC, S)
        ff_gate = [view(big, i * S, S) for i in range(2)]
        ff_out = view(big, 4096, TT, D)

        def feed_forward(name, eng, l):
            for blk in range(FC // 2):
                n = take(name, "ring")
                w = ring_slot(n, KC, 512)
                if name == "pe":
                    eng.wait_ge(w_loaded[n % 2], 16 * (n // 2 + 1))
                for i in range(2):
                    k = 2 * blk + i
                    gb, ub = (2 * k) % 8, (2 * k + 1) % 8
                    if name == "pe":
                        if k >= 4:
                            eng.wait_ge(ff_mult, l * FC + k - 3)
                        for bank, o in ((gb, 0), (ub, 256)):
                            for kk in range(KC):
                                m = T.matmul(ps[:, bank, :], w[:, kk, o + i * P:o + (i + 1) * P], featv[:, kk, :],
                                             start=kk == 0, stop=kk == KC - 1)
                        m.then_inc(ff_full, 1)
                    if name == "act":
                        eng.wait_ge(ff_full, l * FC + k + 1)
                        if k >= 2:
                            eng.wait_ge(ff_mult, l * FC + k - 1)
                        A.activation(ff_gate[k % 2], ps[:, gb, :], ACT.Silu).then_inc(ff_silu, 1)
                    if name == "dve":
                        eng.wait_ge(ff_silu, l * FC + k + 1)
                        V.tensor_tensor(hidden[:, k, :], ff_gate[k % 2], ps[:, ub, :], ALU.mult).then_inc(ff_mult, 1)
                if name == "pe":
                    eng.drain().then_inc(w_used, 1)
            phase(name, eng)
            done_k = 0
            while done_k < FC:
                n = take(name, "ring")
                part = min(4, FC - done_k)
                if name == "pe":
                    w = ring_slot(n, part, D)
                    eng.wait_ge(w_loaded[n % 2], 16 * (n // 2 + 1))
                    for j in range(part):
                        k = done_k + j
                        for t in range(TT):
                            for half in range(2):
                                T.matmul(ps[:, 2 * t + half, :], hidden[:, k, t * P:(t + 1) * P],
                                         w[:, j, half * 512:(half + 1) * 512], start=k == 0, stop=k == FC - 1)
                    eng.drain().then_inc(w_used, 1)
                done_k += part
            phase(name, eng)
            for t in range(TT):
                src = ps[:, 2 * t:2 * t + 2, :].rearrange("p b n -> p (b n)")
                if name == "dve" and t % 2 == 0:
                    V.tensor_copy(ff_out[:, t, :], src)
                if name == "act" and t % 2 == 1:
                    A.activation(ff_out[:, t, :], src, ACT.Copy)
            phase(name, eng)
            add_normed(name, eng, ff_out, p2(l, "ffn_post"))

        def rotary(name, eng):
            two_pi = 6.283185307179586
            c1 = 6.28125
            c2 = 2029.0 / 2 ** 20
            c3 = two_pi - c1 - c2
            n1, n2 = TT * 16, TT * 8
            pos = view(tmp, 0, TT)
            ang = view(tmp, 64, 2 * (n1 + n2))
            turns_i = view(tmp, 512, 2 * (n1 + n2)).bitcast(i32)
            turns = view(tmp, 1024, 2 * (n1 + n2))
            if name == "pool":
                G.memset(stat[:, 255:256], -0.5)
            if name == "dve":
                eng.wait_ge(pos_loaded, 16)
                V.tensor_copy(pos, view(tmp, 16, TT).bitcast(i32))
                eng.drain()
                for o, n, f in ((0, 16, "freq1"), (128, 8, "freq2")):
                    for h in range(2):
                        V.tensor_tensor(view(tmp, 64 + o + h * TT * n, TT, n), pos.unsqueeze(2).to_broadcast([P, TT, n]),
                                        c_(f).unsqueeze(1).to_broadcast([P, TT, n]), ALU.mult)
                eng.drain()
                V.tensor_scalar(turns, ang, 1.0 / two_pi, None, ALU.mult)
                eng.drain()
                V.tensor_copy(turns_i, turns)
                eng.drain()
                V.tensor_copy(turns, turns_i)
                eng.drain()
                for part in (c1, c2, c3):
                    V.scalar_tensor_tensor(out=ang, in0=turns, scalar=-part, in1=ang, op0=ALU.mult, op1=ALU.add)
                    eng.drain()
                for o, n in ((0, n1), (128, n2)):
                    v = view(tmp, 64 + o, n)
                    V.tensor_scalar(v, v, two_pi / 4, None, ALU.add)
                eng.drain()
                for sign in (1.0, -1.0):
                    V.tensor_scalar(turns, ang, sign * two_pi / 2, None, ALU.is_gt if sign > 0 else ALU.is_lt)
                    eng.drain()
                    V.scalar_tensor_tensor(out=ang, in0=turns, scalar=-sign * two_pi, in1=ang, op0=ALU.mult, op1=ALU.add)
                    eng.drain()
                V.tensor_scalar(ang, ang, 3.1415925, -3.1415925, ALU.min, ALU.max)
            phase(name, eng)
            if name == "act":
                A.activation(rope[:, 0:2 * (n1 + n2)], ang, ACT.Sin)
            phase(name, eng)

        moe_phase = []

        def run(name, eng):
            rotary(name, eng)
            if name == "act":
                eng.wait_ge(x_loaded, 16)
                eng.wait_ge(par_loaded[0], 16)
                eng.wait_ge(par_loaded[1], 16)
            phase(name, eng)
            for l in range(LAYERS):
                norm(name, eng, x, view(tmp, 0, TT, D), featv, p1(l, "attn_g"))
                in_projection(name, eng, l)
                conv_and_gates(name, eng, l)
                mlstm(name, eng, l)
                latent_inputs(name, eng, l)
                latent_attention(name, eng, l)
                spatial_gating(name, eng, l)
                heads_out(name, eng, l)
                norm(name, eng, x, xn, featv, p1(l, "ffn_g"))
                share_rows(name, eng, l)
                router(name, eng, l)
                if name == "pe":
                    moe_phase.append((count[("pe", "phase")], count[("pe", "ring")]))
                fill_table(name, eng, l)
                experts(name, eng, l)
                phase(name, eng)
                combine(name, eng, l)
            if name == "pool":
                for i in range(2):
                    eng.dma_start(par[i][:, 0:PAR2_W], a["par2"][i]).then_inc(par2_loaded, 16)
                eng.wait_ge(par2_loaded, 32)
            phase(name, eng)
            for l in range(LAYERS):
                norm(name, eng, x, view(tmp, 0, TT, D), featv, p2(l, "mix_g"))
                mixer(name, eng, l)
                memory_attention(name, eng, l)
                norm(name, eng, x, view(tmp, 0, TT, D), featv, p2(l, "ffn_g"))
                feed_forward(name, eng, l)

        m_staged, m_scores, m_decay_in = sem("m_staged"), sem("m_scores"), sem("m_decay_in")
        m_decayed, m_weighed, m_out = sem("m_decayed"), sem("m_weighed"), sem("m_out")
        d_staged, d_turned, d_qT, d_kT = sem("d_staged"), sem("d_turned"), sem("d_qT"), sem("d_kT")
        d_scores, d_max, d_probs, d_mixed = sem("d_scores"), sem("d_max"), sem("d_probs"), sem("d_mixed")
        d_full, d_probT, d_out, d_read = sem("d_full"), sem("d_probT"), sem("d_out"), sem("d_read")
        ff_full, ff_silu, ff_mult = sem("ff_full"), sem("ff_silu"), sem("ff_mult")

        block = ctx.enter_context(nc.Block())

        @block.tensor
        def _(pe):
            pe.wait_ge(const_loaded, 16)
            for s in range(E_SLOTS):
                pe.sem_inc(e_turned[s], 1)
                pe.sem_inc(e_up[s], 1)
                pe.sem_inc(e_hturned[s], 1)
                pe.sem_inc(e_down[s], 1)
            run("pe", pe)

        @block.vector
        def _(dve):
            dve.wait_ge(const_loaded, 16)
            for s in range(E_SLOTS):
                dve.sem_inc(e_rowsT[s], 1)
                dve.sem_inc(e_hidden[s], 1)
                dve.sem_inc(e_hiddenT[s], 1)
            run("dve", dve)

        @block.scalar
        def _(act):
            for s in range(E_SLOTS):
                act.sem_inc(e_silu[s], 1)
                act.sem_inc(e_copied[s], 1)
                act.dma_start(e_y[s][:, 0:8], a["x"][0:P, 0:8]).then_inc(e_stored[s], 16)
            for s in range(E_SLOTS):
                act.wait_ge(e_stored[s], 16)
            act.dma_start(x, a["x"].rearrange("(t p) d -> p t d", p=P)).then_inc(x_loaded, 16)
            for i in range(2):
                act.dma_start(par[i][:, 0:PAR1_W], a["par1"][i]).then_inc(par_loaded[i], 16)
            run("act", act)

        @block.gpsimd
        def _(pool):
            pool.dma_start(tok_id, a["tok_id"]).then_inc(ids_loaded, 16)
            pool.wait_ge(ids_loaded, 16)
            run("pool", pool)

        @block.sync
        def _(sp):
            sp.dma_start(cst[:, :], a["consts"]).then_inc(const_loaded, 16)
            sp.dma_start(view(tmp, 16, TT).bitcast(i32), a["positions"]).then_inc(pos_loaded, 16)
            n = 0

            def load(src, kc, width):
                nonlocal n
                if n >= 2:
                    sp.wait_ge(w_used, n - 1)
                sp.dma_start(ring_slot(n, kc, width), src).then_inc(w_loaded[n % 2], 16)
                n += 1

            def load_columns(src, widths, kc=KC):
                at = 0
                for width in widths:
                    load(src[:, :, at:at + width], kc, width)
                    at += width

            for l in range(LAYERS):
                load_columns(a["w_qk"][l], [M_WIDTH] * 2)
                load_columns(a["w_tok"][l], [512, 512, 512, TOK_W - 1536])
                load_columns(a["w_out"][l], [512] * 2)
                phases, blocks = moe_phase[l]
                assert blocks == n
                for s in done.values():
                    sp.wait_ge(s, phases)
                experts("sp", sp, l)
                sp.wait_ge(e_down[0], (l + 1) * E_STEPS + 1)
            for l in range(LAYERS):
                load_columns(a["w_mix_in"][l], [512] * 6)
                load_columns(a["w_mix_out"][l], [512] * 2)
                load_columns(a["w_mem_kv"][l], [512] * 4)
                load_columns(a["w_mem_q"][l], [512] * 2)
                load_columns(a["w_mem_o"][l], [512] * 2)
                load_columns(a["w_gate_up"][l], [512] * (FC // 2))
                for k in range(0, FC, 4):
                    load(a["w_down"][l][:, k:min(k + 4, FC), :], min(4, FC - k), D)
            for s in done.values():
                sp.wait_ge(s, count[("pe", "phase")])
            sp.dma_start(a["out"].rearrange("(t p) d -> p t d", p=P), x).then_inc(out_stored, 16)
            sp.wait_ge(out_stored, 16)


def host_layout(inp):
    import numpy as np
    v = {k: np.asarray(t) for k, t in inp.items()}

    def chunks(w):
        l, k, n = w.shape
        return np.ascontiguousarray(w.reshape(l, k // P, P, n).transpose(0, 2, 1, 3))

    def pack(lay, width, parts):
        out = np.zeros((P, width), np.float32)
        for name, p in parts.items():
            o, w = lay[name]
            p = np.asarray(p, np.float32)
            out[0:p.shape[0], o:o + w] = p.reshape(p.shape[0], w)
        return out

    def per_part(vec, n):
        return vec.reshape(-1, n).T

    def rep(vec):
        return np.broadcast_to(vec.reshape(1, -1), (P, vec.size))

    i, j = np.arange(P)[:, None], np.arange(P)[None, :]
    causal = np.zeros((P, S), np.float32)
    causal[:, S - P:] = np.where(j <= i, 0.0, -1e30)
    gap = np.abs((np.arange(TT)[None, :, None] * P + np.arange(P)[:, None, None]) - np.arange(S)[None, None, :])
    times = (gap <= 64) * 1 + ((gap <= 256) & (gap % 4 == 0)) * 1 + (gap % 16 == 0) * 1
    lnc = np.where(times > 0, np.log(np.maximum(times, 1)), -1e30).astype(np.float32)
    pick = np.zeros((M_HEADS, M_HEADS, P), np.float32)
    for h in range(M_HEADS):
        pick[h, h] = 1.0
    f1 = (1.0 / (np.float32(10000.0) ** (np.arange(0, A_ROPE, 2, dtype=np.float32) / np.float32(A_ROPE)))).astype(np.float32)
    f2 = (np.float32(500000.0) ** (-np.arange(0, ROT, 2, dtype=np.float32) / np.float32(ROT))).astype(np.float32)
    consts = pack(CONSTS, CONST_W, dict(
        ident=np.eye(P), ones=np.ones((P, P)), before=(i < j) * 1.0, upto=(i <= j) * 1.0, causal=causal,
        dilated=lnc, iota=rep(np.arange(N_EXP)), blocks=rep(np.arange(N_BLK)), pick=pick, freq1=rep(f1), freq2=rep(f2)))

    w_in = v["w_in"]
    cut = np.cumsum([0, 384, 384, 384, 384, 4, 4, 256, 128, 32, 256, 256])
    mq, mk, mv, mo, mi, mf, cq, ckv, kr, cu, cv = (w_in[:, :, s:e] for s, e in zip(cut[:-1], cut[1:]))
    mv = np.concatenate([mv.reshape(LAYERS, D, M_HEADS, M_DIM), np.zeros((LAYERS, D, M_HEADS, 1), np.float32)], axis=3)
    w_tok = np.concatenate([mv.reshape(LAYERS, D, -1), mo, cq, ckv, kr, cu, cv], axis=2)

    par1 = []
    for l in range(LAYERS):
        par1.append(pack(PAR1, PAR1_W, dict(
            attn_g=per_part(v["attn_norm"][l], P),
            conv_w=v["m_conv_w"][l].reshape(CONV, QK_TILES, M_DIM).transpose(2, 1, 0),
            conv_b=per_part(v["m_conv_b"][l], M_DIM),
            gate_b=v["m_gate_bias"][l].reshape(2, M_HEADS).T,
            cq_g=per_part(v["a_q_norm"][l], P), ckv_g=per_part(v["a_kv_norm"][l], P),
            qh_g=rep(v["a_q_head_norm"][l]), kh_g=rep(v["a_k_head_norm"][l]), cv_g=rep(v["c_v_norm"][l]),
            w_s=v["c_w_s"][l].transpose(2, 0, 1), b_s=v["c_b_s"][l].T,
            out_g=per_part(v["mix_out_norm"][l], P), ffn_g=per_part(v["ffn_norm"][l], P),
            group_b=rep(v["b_group"][l]), exp_b=rep(v["b_expert"][l]),
            w_gate=chunks(np.concatenate([mi, mf], axis=2))[l],
            w_uq=chunks(v["a_w_uq"])[l], w_ukv=chunks(v["a_w_ukv"])[l],
            w_route=chunks(np.concatenate([v["w_group"], v["w_expert"]], axis=2))[l])))
    par2 = []
    lam = np.concatenate([v[k].reshape(-1) for k in ("b_lam_q1_2", "b_lam_k1_2", "b_lam_q2_2", "b_lam_k2_2")])
    for l in range(LAYERS):
        par2.append(pack(PAR2, PAR2_W, dict(
            mix_g=per_part(v["mix_pre_g_2"][l], P), mem_g=per_part(v["mem_pre_g_2"][l], P),
            memkv_g=per_part(v["mem_kv_g_2"][l], P), ffn_g=per_part(v["ffn_pre_g_2"][l], P),
            mix_post=rep(v["mix_post_g_2"][l]), mem_post=rep(v["mem_post_g_2"][l]), ffn_post=rep(v["ffn_post_g_2"][l]),
            sub_g=v["b_sub_g_2"].reshape(P, 1), lam=rep(lam))))

    w13 = np.concatenate([v["w1"], v["w3"]], axis=3).reshape(LAYERS, N_EXP, KC, P, 2 * D_EXP)
    w13 = np.ascontiguousarray(w13.transpose(0, 1, 3, 2, 4)).reshape(LAYERS, N_EXP, P, -1)
    w2 = v["w2"].reshape(LAYERS, N_EXP, 2, P, D).transpose(0, 1, 3, 2, 4)
    gu = v["w_gate_up_2"].reshape(LAYERS, D, 2, FF // 256, 256).transpose(0, 1, 3, 2, 4).reshape(LAYERS, D, 2 * FF)
    return dict(
        x=np.ascontiguousarray(v["x"].reshape(S, D)),
        positions=np.ascontiguousarray(v["positions"].reshape(TT, P).T.astype(np.int32)),
        tok_id=np.ascontiguousarray(np.arange(S, dtype=np.int32).reshape(TT, P).T),
        consts=consts, par1=np.stack(par1), par2=np.stack(par2),
        w_qk=chunks(np.concatenate([mq, mk], axis=2)), w_tok=chunks(w_tok), w_out=chunks(v["w_out"]),
        w13=w13, w2=np.ascontiguousarray(w2).reshape(LAYERS, N_EXP, P, -1),
        mem=np.ascontiguousarray(v["mem_2"].reshape(N_MEM, D)),
        w_mix_in=chunks(np.concatenate([v["a_w_in_2"], v["b_w_in_2"]])),
        w_mix_out=chunks(np.concatenate([v["a_w_out_2"], v["b_w_out_2"]])),
        w_mem_kv=chunks(v["x_wkv_2"]), w_mem_q=chunks(v["x_wq_2"]), w_mem_o=chunks(v["x_wo_2"]),
        w_gate_up=chunks(gu), w_down=chunks(v["w_down_2"]))


def kernel(**inputs):
    import numpy as np
    import concourse.bacc as bacc
    from concourse.bass_utils import run_bass_kernel_spmd

    arrays = host_layout(inputs)
    nc = bacc.Bacc("TRN2", target_bir_lowering=False, num_devices=1)
    args = {k: nc.dram_tensor(f"in_{k}", t.shape, mybir.dt.from_np(t.dtype), kind="ExternalInput").ap()
            for k, t in arrays.items()}
    args["out"] = nc.dram_tensor("out_0", (S, D), mybir.dt.float32, kind="ExternalOutput").ap()
    for name, shape, dt in (("normed", (S, D), mybir.dt.float32), ("slot_table", (P * TABLE_W,), mybir.dt.int32),
                            ("expert_out", (N_BLK * P, D), mybir.dt.float32)):
        args[name] = nc.dram_tensor(name, shape, dt).ap()
    program(nc, args)
    r = run_bass_kernel_spmd(nc, [{f"in_{k}": t for k, t in arrays.items()}], core_ids=[0])
    return r.results[0]["out_0"].reshape(1, S, D)
```
